# Optimizing a Trainium2 kernel written in Bass

```python
import jax, jax.numpy as jnp
from jax import lax
import numpy as np

D_MODEL = 1024
BATCH = 1
SEQ = 128
DEPTH = 1
DEC_BATCH = 1
DEC_SEQ = 256
PAST_LEN = 128

GRID_W = 64
HEAD_DIM = 64
ATTN_HEADS = 8
KV_HEADS = 2
GQA_GROUP = ATTN_HEADS // KV_HEADS
ATTN_WIDTH = ATTN_HEADS * HEAD_DIM
KV_WIDTH = KV_HEADS * HEAD_DIM
ATTN_IN = ATTN_WIDTH + 2 * KV_WIDTH
ATTN_SCALE = HEAD_DIM ** -0.5
Q_BLOCK = 128
ROPE_THETA = 10000.0
ROPE_HALF = HEAD_DIM // 2
ROPE_FREQS = ROPE_HALF // 2
RWKV_HEAD = 64
RWKV_HEADS = 8
RWKV_WIDTH = RWKV_HEADS * RWKV_HEAD
DECAY_RANK = 64
ICLR_RANK = 64
GATE_RANK = 128
RWKV_SIZES = (RWKV_WIDTH, RWKV_WIDTH, RWKV_WIDTH, DECAY_RANK, DECAY_RANK, ICLR_RANK, ICLR_RANK, GATE_RANK)
RWKV_IN = 3 * RWKV_WIDTH + 2 * DECAY_RANK + 2 * ICLR_RANK + GATE_RANK
D_IN = ATTN_IN + RWKV_IN
MIX_WIDTH = ATTN_WIDTH + RWKV_WIDTH
DECAY_SCALE = 0.606531
GN_EPS = 64e-5
N_EXPERTS = 64
TOP_K = 6
N_GROUPS = 8
TOPK_GROUPS = 4
EXPERT_FF = 256
SHARED_FF = 256
ROUTED_SCALE = 2.5
EPS = 1e-6

kernel_name = 'hybrid_attn_rwkv7_moe_diffusion_step'

f32 = jnp.float32

def _split_cols(z, sizes):
    offs = np.cumsum(sizes)[:-1].tolist()
    return jnp.split(z, offs, axis=-1)

def rmsnorm(x, g):
    xf = x.astype(f32)
    y = xf * lax.rsqrt(jnp.mean(xf * xf, axis=-1, keepdims=True) + EPS) * g.astype(f32)
    return y.astype(x.dtype)

def axial_rope(row_idx, col_idx):
    inv = ROPE_THETA ** (-jnp.arange(0, ROPE_HALF, 2, dtype=f32) / ROPE_HALF)
    ang = jnp.stack([row_idx.astype(f32)[:, None] * inv, col_idx.astype(f32)[:, None] * inv], axis=1)
    ang = ang[:, None, :, None, :]
    return jnp.cos(ang), jnp.sin(ang)

def apply_rope(x, cos, sin):
    xs = x.reshape(x.shape[:-1] + (2, 2, ROPE_FREQS))
    rot = jnp.stack([-xs[..., 1, :], xs[..., 0, :]], axis=-2)
    out = xs * cos.astype(x.dtype) + rot * sin.astype(x.dtype)
    return out.reshape(x.shape)

def block_attention(q, k, v):
    B, T, H, D = q.shape
    nb = T // Q_BLOCK
    qb = q.reshape(B, nb, Q_BLOCK, KV_HEADS, GQA_GROUP, D).transpose(1, 0, 2, 3, 4, 5)

    def one(qblk):
        s = jnp.einsum('bqkgd,blkd->bkgql', qblk, k).astype(f32) * ATTN_SCALE
        p = jax.nn.softmax(s, axis=-1).astype(v.dtype)
        return jnp.einsum('bkgql,blkd->bqkgd', p, v)

    o = lax.map(one, qb)
    return o.transpose(1, 0, 2, 3, 4, 5).reshape(B, T, H * D)

def token_shift(z, mu_prev, mu_next):
    prev = jnp.pad(z[:, :-1], ((0, 0), (1, 0), (0, 0)))
    nxt = jnp.pad(z[:, 1:], ((0, 0), (0, 1), (0, 0)))
    return z + mu_prev * (prev - z) + mu_next * (nxt - z)

def _wkv_step(S, inp):
    w, kk, b, k, r, v = inp
    sa = jnp.einsum('dbhvk,dbhk->dbhv', S, -kk)
    S = S * w[..., None, :] + sa[..., :, None] * b[..., None, :] + v[..., :, None] * k[..., None, :]
    return S, jnp.einsum('dbhvk,dbhk->dbhv', S, r)

def rwkv_mix(z_rwkv, p, s0):
    zs = token_shift(z_rwkv, p['mu_prev'], p['mu_next'])
    r, k, v, dw_f, dw_b, da_f, da_b, dg = _split_cols(zs, RWKV_SIZES)
    B, T, _ = r.shape
    dw = jnp.stack([dw_f, dw_b])
    da = jnp.stack([da_f, da_b])
    w_raw = p['decay_w0'][:, None, None, :] + jnp.einsum('dbtr,drc->dbtc', jnp.tanh(dw), p['decay_w2'])
    decay = jnp.exp(-DECAY_SCALE * jax.nn.sigmoid(w_raw.astype(f32)))
    a = jax.nn.sigmoid((p['iclr_a0'][:, None, None, :] + jnp.einsum('dbtr,drc->dbtc', da, p['iclr_a2'])).astype(f32))
    g = (jax.nn.sigmoid(dg) @ p['gate_g2']).astype(f32)

    def heads(t):
        return t.reshape(t.shape[:-1] + (RWKV_HEADS, RWKV_HEAD))

    rf, kf, vf = r.astype(f32), k.astype(f32), v.astype(f32)
    kk = heads(kf * p['k_k'].astype(f32))
    kk = kk * lax.rsqrt(jnp.sum(kk * kk, axis=-1, keepdims=True) + 1e-12)
    k_eff = heads(kf[None] * (1.0 + (a - 1.0) * p['k_a'].astype(f32)))
    b = kk[None] * heads(a)
    rh, vh = heads(rf), heads(vf)

    def to_scan(t):
        t = jnp.stack([t[0], jnp.flip(t[1], axis=1)])
        return jnp.moveaxis(t, 2, 0)

    def both(t):
        return jnp.broadcast_to(t[None], (2,) + t.shape)

    xs = (to_scan(heads(decay)), to_scan(both(kk)), to_scan(b), to_scan(k_eff), to_scan(both(rh)), to_scan(both(vh)))
    s_fin, o = lax.scan(_wkv_step, s0.astype(f32), xs)
    o = jnp.moveaxis(o, 0, 2)
    o = o[0] + jnp.flip(o[1], axis=1)
    mu = jnp.mean(o, axis=-1, keepdims=True)
    var = jnp.mean(jnp.square(o - mu), axis=-1, keepdims=True)
    on = ((o - mu) * lax.rsqrt(var + GN_EPS)).reshape(B, T, RWKV_WIDTH)
    on = on * p['lnx_g'].astype(f32) + p['lnx_b'].astype(f32)
    bonus = jnp.sum(jnp.sum(rh[None] * k_eff * p['r_k'].astype(f32), axis=-1, keepdims=True), axis=0) * vh
    out = (on + bonus.reshape(B, T, RWKV_WIDTH)) * g
    return out.astype(z_rwkv.dtype), s_fin.astype(z_rwkv.dtype)

def mixer(h, p, rope, past_k, past_v, s0):
    B, T, _ = h.shape
    z = h @ p['w_in']
    z_attn, z_rwkv = z[..., :ATTN_IN], z[..., ATTN_IN:]
    q, k, v = _split_cols(z_attn, (ATTN_WIDTH, KV_WIDTH, KV_WIDTH))
    q = rmsnorm(q.reshape(B, T, ATTN_HEADS, HEAD_DIM), p['q_gain'])
    k = rmsnorm(k.reshape(B, T, KV_HEADS, HEAD_DIM), p['k_gain'])
    v = v.reshape(B, T, KV_HEADS, HEAD_DIM)
    k_own, v_own = k, v
    if rope is not None:
        q = apply_rope(q, *rope)
        k = jnp.concatenate([past_k.astype(k.dtype), apply_rope(k, *rope)], axis=1)
        v = jnp.concatenate([past_v.astype(v.dtype), v], axis=1)
    attn = block_attention(q, k, v)
    rw, s_fin = rwkv_mix(z_rwkv, p, s0)
    y = jnp.concatenate([attn, rw], axis=-1) @ p['w_out']
    return y, k_own, v_own, s_fin

def moe(h, p):
    x2 = h.reshape(-1, h.shape[-1])
    n = x2.shape[0]
    scores = jax.nn.sigmoid((x2 @ p['router_w']).astype(f32))
    biased = scores + p['router_b'].astype(f32)
    grp = biased.reshape(n, N_GROUPS, N_EXPERTS // N_GROUPS)
    grp_score = jnp.sum(lax.top_k(grp, 2)[0], axis=-1)
    _, gidx = lax.top_k(grp_score, TOPK_GROUPS)
    gmask = jnp.sum(jax.nn.one_hot(gidx, N_GROUPS, dtype=f32), axis=-2)
    emask = jnp.repeat(gmask, N_EXPERTS // N_GROUPS, axis=-1)
    _, eidx = lax.top_k(jnp.where(emask > 0, biased, -jnp.inf), TOP_K)
    wsel = jnp.take_along_axis(scores, eidx, axis=-1)
    wsel = wsel / jnp.sum(wsel, axis=-1, keepdims=True) * ROUTED_SCALE
    gates = jnp.sum(jax.nn.one_hot(eidx, N_EXPERTS, dtype=f32) * wsel[..., None], axis=-2).astype(h.dtype)

    def expert(acc, e):
        wg, wu, wd, ge = e
        y = (jax.nn.silu(x2 @ wg) * (x2 @ wu)) @ wd
        return acc + ge[:, None] * y, None

    routed, _ = lax.scan(expert, jnp.zeros_like(x2), (p['expert_wg'], p['expert_wu'], p['expert_wd'], gates.T))
    shared = (jax.nn.silu(x2 @ p['shared_wg']) * (x2 @ p['shared_wu'])) @ p['shared_wd']
    return (routed + shared).reshape(h.shape)

def trunk_layer(x, mod, p, rope, past_k, past_v, s0):
    sh_a, sc_a, gt_a, sh_f, sc_f, gt_f = jnp.split(mod, 6, axis=-1)
    h = rmsnorm(x, p['g_pre_mix']) * (1 + sc_a) + sh_a
    y, kc, vc, st = mixer(h, p, rope, past_k, past_v, s0)
    x = x + gt_a * rmsnorm(y, p['g_post_mix'])
    h = rmsnorm(x, p['g_pre_ffn']) * (1 + sc_f) + sh_f
    x = x + gt_f * rmsnorm(moe(h, p), p['g_post_ffn'])
    return x, kc, vc, st

def setup_inputs(seed: int = 0) -> dict:
    key = jax.random.key(seed)
    ks = iter(jax.random.split(key, 48))
    nrm = lambda shape, s=1.0: jax.random.normal(next(ks), shape, f32) * s
    gain = lambda shape: 1.0 + 0.02 * jax.random.normal(next(ks), shape, f32)
    L = DEPTH
    return {
        'x_prompt': nrm((BATCH, SEQ, D_MODEL)),
        'x_sample': nrm((DEC_BATCH, DEC_SEQ, D_MODEL)),
        'c': nrm((DEC_BATCH, D_MODEL)),
        'cache_k': nrm((DEC_BATCH, L, PAST_LEN, KV_HEADS, HEAD_DIM)),
        'cache_v': nrm((DEC_BATCH, L, PAST_LEN, KV_HEADS, HEAD_DIM)),
        'state_rwkv': nrm((DEC_BATCH, L, 2, RWKV_HEADS, RWKV_HEAD, RWKV_HEAD)),
        'c_ctx': nrm((D_MODEL,)),
        'w_ada': nrm((L, D_MODEL, 6 * D_MODEL), 0.5 * D_MODEL ** -0.5),
        'b_ada': nrm((L, 6 * D_MODEL), 0.01),
        'g_pre_mix': gain((L, D_MODEL)),
        'g_post_mix': gain((L, D_MODEL)),
        'g_pre_ffn': gain((L, D_MODEL)),
        'g_post_ffn': gain((L, D_MODEL)),
        'w_in': nrm((L, D_MODEL, D_IN), D_MODEL ** -0.5),
        'w_out': nrm((L, MIX_WIDTH, D_MODEL), MIX_WIDTH ** -0.5),
        'q_gain': gain((L, HEAD_DIM)),
        'k_gain': gain((L, HEAD_DIM)),
        'mu_prev': jax.random.uniform(next(ks), (L, RWKV_IN), f32, 0.0, 0.5),
        'mu_next': jax.random.uniform(next(ks), (L, RWKV_IN), f32, 0.0, 0.5),
        'decay_w0': nrm((L, 2, RWKV_WIDTH)),
        'decay_w2': nrm((L, 2, DECAY_RANK, RWKV_WIDTH), DECAY_RANK ** -0.5),
        'iclr_a0': nrm((L, 2, RWKV_WIDTH), 0.5),
        'iclr_a2': nrm((L, 2, ICLR_RANK, RWKV_WIDTH), ICLR_RANK ** -0.5),
        'gate_g2': nrm((L, GATE_RANK, RWKV_WIDTH), GATE_RANK ** -0.5),
        'k_k': 0.85 + nrm((L, RWKV_WIDTH), 0.02),
        'k_a': gain((L, RWKV_WIDTH)),
        'r_k': nrm((L, RWKV_HEADS, RWKV_HEAD), 0.1),
        'lnx_g': gain((L, RWKV_WIDTH)),
        'lnx_b': nrm((L, RWKV_WIDTH), 0.01),
        'router_w': nrm((L, D_MODEL, N_EXPERTS), D_MODEL ** -0.5),
        'router_b': nrm((L, N_EXPERTS), 0.01),
        'expert_wg': nrm((L, N_EXPERTS, D_MODEL, EXPERT_FF), D_MODEL ** -0.5),
        'expert_wu': nrm((L, N_EXPERTS, D_MODEL, EXPERT_FF), D_MODEL ** -0.5),
        'expert_wd': nrm((L, N_EXPERTS, EXPERT_FF, D_MODEL), EXPERT_FF ** -0.5),
        'shared_wg': nrm((L, D_MODEL, SHARED_FF), D_MODEL ** -0.5),
        'shared_wu': nrm((L, D_MODEL, SHARED_FF), D_MODEL ** -0.5),
        'shared_wd': nrm((L, SHARED_FF, D_MODEL), SHARED_FF ** -0.5),
    }

def reference(x_prompt, x_sample, c, cache_k, cache_v, state_rwkv, c_ctx, w_ada, b_ada,
              g_pre_mix, g_post_mix, g_pre_ffn, g_post_ffn, w_in, w_out, q_gain, k_gain,
              mu_prev, mu_next, decay_w0, decay_w2, iclr_a0, iclr_a2, gate_g2, k_k, k_a, r_k,
              lnx_g, lnx_b, router_w, router_b, expert_wg, expert_wu, expert_wd,
              shared_wg, shared_wu, shared_wd):
    rows = x_sample.shape[1] // GRID_W
    row_idx = jnp.repeat(jnp.arange(rows, dtype=jnp.int32), GRID_W)
    col_idx = jnp.tile(jnp.arange(GRID_W, dtype=jnp.int32), rows)
    rope = axial_rope(row_idx, col_idx)
    n_ctx = x_prompt.shape[0]
    y_p, y_s = x_prompt, x_sample
    ks_out, vs_out, st_out = [], [], []
    for l in range(DEPTH):
        p = {
            'g_pre_mix': g_pre_mix[l], 'g_post_mix': g_post_mix[l],
            'g_pre_ffn': g_pre_ffn[l], 'g_post_ffn': g_post_ffn[l],
            'w_in': w_in[l], 'w_out': w_out[l], 'q_gain': q_gain[l], 'k_gain': k_gain[l],
            'mu_prev': mu_prev[l], 'mu_next': mu_next[l],
            'decay_w0': decay_w0[l], 'decay_w2': decay_w2[l],
            'iclr_a0': iclr_a0[l], 'iclr_a2': iclr_a2[l], 'gate_g2': gate_g2[l],
            'k_k': k_k[l], 'k_a': k_a[l], 'r_k': r_k[l], 'lnx_g': lnx_g[l], 'lnx_b': lnx_b[l],
            'router_w': router_w[l], 'router_b': router_b[l],
            'expert_wg': expert_wg[l], 'expert_wu': expert_wu[l], 'expert_wd': expert_wd[l],
            'shared_wg': shared_wg[l], 'shared_wu': shared_wu[l], 'shared_wd': shared_wd[l],
        }
        mod_ctx = (jax.nn.silu(c_ctx)[None] @ w_ada[l] + b_ada[l])[:, None, :]
        mod_lat = (jax.nn.silu(c) @ w_ada[l] + b_ada[l])[:, None, :]
        s0_ctx = jnp.zeros((2, n_ctx, RWKV_HEADS, RWKV_HEAD, RWKV_HEAD), f32)
        y_p, kc, vc, st = trunk_layer(y_p, mod_ctx, p, None, None, None, s0_ctx)
        ks_out.append(kc)
        vs_out.append(vc)
        st_out.append(jnp.moveaxis(st, 0, 1))
        s0_lat = jnp.moveaxis(state_rwkv[:, l], 1, 0)
        y_s, _, _, _ = trunk_layer(y_s, mod_lat, p, rope, cache_k[:, l], cache_v[:, l], s0_lat)
    new_cache_k = jnp.stack(ks_out, axis=1)
    new_cache_v = jnp.stack(vs_out, axis=1)
    new_state_rwkv = jnp.stack(st_out, axis=1)
    return (y_prompt := y_p, y_s, new_cache_k, new_cache_v, new_state_rwkv)


_drawn_inputs = setup_inputs


def setup_inputs(seed=0):
    import zlib

    import numpy as np

    out = dict(_drawn_inputs(seed))
    spreads = {}
    factors = {'g_post_mix': 2.785,
     'g_post_ffn': 8.0,
     'q_gain': 6.611,
     'k_k': 3.848,
     'lnx_g': 3.426,
     'lnx_b': 3.524}
    for name, (base, spread) in spreads.items():
        noise = np.random.default_rng([zlib.crc32(name.encode()), seed]).standard_normal(out[name].shape)
        drawn = base * np.exp(spread * noise) if base else spread * noise
        out[name] = __import__('jax').numpy.asarray(drawn.astype(out[name].dtype))
    for name, factor in factors.items():
        out[name] = (out[name] * factor).astype(out[name].dtype)
    return out
```

```python
from contextlib import ExitStack

import numpy as np

import concourse.bass as bass
from concourse import mybir

F32 = mybir.dt.float32
I32 = mybir.dt.int32
U32 = mybir.dt.uint32
ALU = mybir.AluOpType
ACT = mybir.ActivationFunctionType
AX = mybir.AxisListType

P = 128
D = 1024
KC = D // P
TT = 3
T = TT * P
NQ = 4
AIN = 768
NCH = 4
NZ = 15
DECAY_SCALE = 0.606531
GN_EPS = 64e-5
EPS = 1e-6
LEVELS = (2, 4, 8, 16, 32, 64)
E_N = 64
TOP_K = 6
ROUTED_SCALE = 2.5
FF = 256
BIG = 1 << 20
NB = E_N // 4
OVER = P * E_N

C_GPRE, C_QG, C_KG, C_MP, C_MN, C_W0, C_A0, C_KK, C_KA, C_RK = 0, 8, 9, 10, 25, 40, 48, 56, 60, 64
C_N = 68

CONSTS = [("ident", P), ("blk", P), ("nm0", P), ("nm1", P), ("st0", P), ("st1", P), ("in0", P),
          ("in1", P), ("ones", P), ("hm0", 384), ("hm1", 384), ("bones", 2), ("nscale", 1),
          ("nbias", 1), ("eps", 1), ("gneps", 1)]
EARLY = [("cos", T), ("sin", T), ("rot", P), ("dup0", P), ("dup1", P), ("hsum", 9 * 18), ("hbc", 9 * P)]


def offsets(parts):
    out, at = {}, 0
    for name, n in parts:
        out[name] = (at, n)
        at += n
    return out, at


OFF_C, N_C = offsets(CONSTS)
OFF_E, N_E = offsets(EARLY)


def constant_arrays():
    i = np.arange(P)
    row, col = i[:, None], i[None, :]
    c = {}
    c["ident"] = (row == col)
    c["blk"] = (row // 64 == col // 64)
    c["nm0"] = -1.0 * ((col == row + 1) & (row % 2 == 0))
    c["nm1"] = -1.0 * ((row == col + 1) & (col % 2 == 0))
    c["st0"], c["st1"] = row < col, row > col
    c["in0"], c["in1"] = row <= col, row >= col
    c["ones"] = np.ones((P, P))
    for d in range(2):
        m = np.zeros((P, len(LEVELS), 64))
        for l, s in enumerate(LEVELS):
            cols = [j for j in range(P) if (j // s) % 2 == d]
            for n, j in enumerate(cols):
                m[:, l, n] = (i // s) == (j // s + (1 if d == 0 else -1))
        c[f"hm{d}"] = m.reshape(P, -1)
    c["bones"] = np.stack([i < 64, i >= 64], 1)
    c["nscale"] = np.where(i < 10, 1.0 / 64, 1.0)[:, None]
    c["nbias"] = np.where(i < 10, EPS, 1e-12)[:, None]
    c["eps"] = np.full((P, 1), EPS)
    c["gneps"] = np.full((P, 1), GN_EPS)
    main = np.concatenate([np.asarray(c[n], np.float32).reshape(P, -1) for n, _ in CONSTS], 1)

    e = {}
    inv = (np.float32(10000.0) ** (-np.arange(0, 32, 2, dtype=np.float32) / np.float32(32))).astype(np.float32)
    t = np.arange(256)
    ang = np.stack([(t // 64).astype(np.float32)[:, None] * inv, (t % 64).astype(np.float32)[:, None] * inv], 1)
    ch = i % 64
    cos, sin = np.ones((P, T)), np.zeros((P, T))
    cos[:, P:] = np.cos(ang)[:, ch // 32, ch % 16].T
    sin[:, P:] = np.sin(ang)[:, ch // 32, ch % 16].T
    e["cos"], e["sin"] = cos, sin
    rot = np.zeros((P, P))
    for m in range(P):
        if m % 32 < 16:
            rot[m + 16, m] = -1.0
        else:
            rot[m - 16, m] = 1.0
    e["rot"] = rot
    for kv in range(2):
        e[f"dup{kv}"] = 0.125 * (row == kv * 64 + col % 64)
    hs = np.zeros((P, 9, 18))
    hb = np.zeros((P, 9, P))
    for j in range(9):
        for h in range(2):
            hs[64 * h:64 * h + 64, j, 2 * j + h] = 1.0
            hb[2 * j + h, j, 64 * h:64 * h + 64] = 1.0
    e["hsum"], e["hbc"] = hs, hb
    early = np.concatenate([np.asarray(e[n], np.float32).reshape(P, -1) for n, _ in EARLY], 1)
    return np.ascontiguousarray(main), np.ascontiguousarray(early)


Z_ORDER = [10, 11, 12, 13, 14, 5, 6, 7, 8, 9, 0, 1, 2, 3, 4]
CHUNKS = [(AIN + 10 * P, 5), (AIN + 5 * P, 5), (AIN, 5), (0, 6)]
I_DI, I_ATT, I_V, I_END = 15, 31, 36, 37
BLOCKS = ((0, 1, 2), (0, 2, 1))


def rep(ap, n):
    return ap.unsqueeze(1).to_broadcast([ap.shape[0], n, ap.shape[1]])


def wide(ap, n):
    return ap.unsqueeze(2).to_broadcast([ap.shape[0], ap.shape[1], n])


def program(nc, A, O):
    ctx = ExitStack()
    with ctx:
        def sb(name, cols, dt=F32, parts=P):
            return ctx.enter_context(nc.sbuf_tensor(name, [parts, cols], dt))

        names = {}

        def sem(name):
            if name not in names:
                names[name] = ctx.enter_context(nc.semaphore(name))
            return names[name]

        ps = ctx.enter_context(nc.psum_tensor("ps", [P, 8, 512], F32))

        const = sb("const", N_C)
        early = sb("early", N_E + 1536)
        col = sb("col", C_N)
        modrow = sb("modrow", 2 * 512)
        adarow = sb("adarow", 2 * 1024)
        small = sb("small", 685)
        arena = sb("arena", 43312)

        def cst(n):
            o, w = OFF_C[n]
            return const[:, o:o + w]

        def erl(n):
            o, w = OFF_E[n]
            return early[:, o:o + w]

        def ar(at, n):
            return arena[:, at:at + n]

        def sm(at, n=1):
            return small[:, at:at + n]

        w2d, w2a, g2 = (early[:, N_E + 512 * i:N_E + 512 * i + 512] for i in range(3))
        res = early[:, 0:3 * D].rearrange("p (t n) -> p t n", t=TT)

        R3, R4 = 21552, 33840
        chunk_at = [0, 5120, 10240, 15360]
        wdec = ar(0, 3072).rearrange("p (a t) -> p a t", a=8)
        aic = ar(3072, 3072).rearrange("p (a t) -> p a t", a=8)
        Ebuf = ar(6144, 3096).rearrange("p (a b t) -> p a b t", a=8, b=3)
        Ibuf = ar(9240, 3096).rearrange("p (a b t) -> p a b t", a=8, b=3)
        raw = ar(12336, 1920).rearrange("p (a t) -> p a t", a=5)
        sq9 = ar(18480, 3456).rearrange("p (a t) -> p a t", a=9)
        X = [ar(1024 * d, 1024).rearrange("p (u t) -> p u t", u=8) for d in range(2)]
        LT = [ar(2048 + 1024 * d, 1024).rearrange("p (u t) -> p u t", u=8) for d in range(2)]
        Y = [ar(4096 + 1024 * d, 1024).rearrange("p (u t) -> p u t", u=8) for d in range(2)]
        MT = [ar(6144 + 1024 * d, 1024).rearrange("p (u t) -> p u t", u=8) for d in range(2)]
        RB = [ar(8192 + 1024 * d, 1024).rearrange("p (u t) -> p u t", u=8) for d in range(2)]
        RK = [ar(10240 + 1024 * d, 1024).rearrange("p (u t) -> p u t", u=8) for d in range(2)]
        Ws = [ar(2048 + 1024 * d, 512) for d in range(2)]
        Us = [ar(1024 * d, 512) for d in range(2)]
        Vtok = ar(12336, 1536).rearrange("p (t n) -> p t n", t=3)
        gtok = ar(13872, 1536).rearrange("p (t n) -> p t n", t=3)
        Obuf = ar(15408, 1536).rearrange("p (t n) -> p t n", t=3)
        tmp = [ar(15408 + 384 * i, 384) for i in range(2)]
        kkb = ar(16944, 1536).rearrange("p (a t) -> p a t", a=4)
        Pb = ar(18480, 1536).rearrange("p (a t) -> p a t", a=4)
        PTb = ar(20016, 1536).rearrange("p (a t) -> p a t", a=3)
        Hs = [ar(18480 + 512 * d, 512).rearrange("p (u t) -> p u t", u=8) for d in range(2)]
        Sp = [ar(19504 + 512 * d, 512).rearrange("p (j t) -> p j t", j=4) for d in range(2)]
        bktok = [ar(s, 1024).rearrange("p (a t) -> p a t", a=8) for s in (20528, 16944)]
        rwT = ar(18480, 1536).rearrange("p (a t) -> p a t", a=4)
        ring = [ar(R3 + 4096 * i, 4096).rearrange("p (c n) -> p c n", c=KC) for i in range(3)]
        aM, bM, kM, rM = (ar(R3 + 3072 * i, 3072).rearrange("p (a t) -> p a t", a=8) for i in range(4))
        xin = ar(R4, 3072).rearrange("p (t n) -> p t n", t=3)
        zs = ar(R4, 5760).rearrange("p (a t) -> p a t", a=NZ)
        SD = [ar(R4 + 512 * d, 512).rearrange("p (j t) -> p j t", j=4) for d in range(2)]
        stout = [ar(R4 + 1024 + 512 * d, 512).rearrange("p (j t) -> p j t", j=4) for d in range(2)]
        hT = ar(R4 + 5760, 3072).rearrange("p (c t) -> p c t", c=KC)
        qr = ar(R4 + 5760, 1536).rearrange("p (a t) -> p a t", a=4)
        attnT = qr
        kall = ar(R4 + 7296, 512)
        kdup = ar(R4 + 7808, 1024).rearrange("p (a t) -> p a t", a=2)
        vown = ar(R4 + 8832, 384).rearrange("p (a t) -> p a t", a=3)
        ck, cv = (ar(R4 + 9216 + P * i, P) for i in range(2))
        kown = ck
        woA = ar(0, 4096).rearrange("p (c n) -> p c n", c=4)
        woR = ar(R4, 4096).rearrange("p (c n) -> p c n", c=4)
        lnx = ar(R4 + 4608, 1024).rearrange("p (a n) -> p a n", a=2)
        MB = ar(4096, 6144).rearrange("p (a s n) -> p a s n", a=3, s=2)
        h2 = ar(12336, 3072).rearrange("p (t n) -> p t n", t=3)
        h2T = ar(15408, 3072).rearrange("p (c t) -> p c t", c=KC)
        wtmp = ar(R4 + 4096, 512)

        csil = sm(0, 16).rearrange("p (c s) -> p c s", s=2)
        cvec = sm(16, 16)
        mcol = sm(32, 32).rearrange("p (a s c) -> p a s c", a=2, s=2)
        Acol = sm(64, 16).rearrange("p (s c) -> p s c", s=2)
        ss, rstd = sm(80, 3), sm(83, 3)
        c1, ka1 = sm(86, 15), sm(101, 4)
        nmx, rsum = sm(105, 4), sm(109, 4)
        scS, scE = sm(113, 24), sm(137, 24)
        rc = sm(161, 24)
        bon = sm(185, 24).rearrange("p (t h) -> p t h", t=3)
        gst = sm(209, 48)
        ssy, ry = sm(257, 3), sm(260, 3)
        ssh = sm(263, 6)
        rs18 = small[0:18, 300:684]
        zero = sm(684).to_broadcast([P, P])

        mod_d = nc.dram_tensor("mod_scratch", [2, 6 * D], F32).ap()
        h2_d = nc.dram_tensor("h2_scratch", [T, D], F32).ap()

        slot_at = [21552, 0, 12288, 27696]
        slot13 = [ar(s, 4096) for s in slot_at]
        slotd = [ar(s + 4096, 2048) for s in slot_at]

        def s13(u):
            return slot13[u].rearrange("p (c n) -> p c n", c=KC)

        def sd(u):
            return slotd[u].rearrange("p (c n) -> p c n", c=2)

        xg = [ar(s, D) for s in (6144, 7168, 18480, 19504)]
        xgT = [ar(8192 + D * i, D).rearrange("p (c t) -> p c t", c=KC) for i in range(2)]
        yb = [ar(10240 + D * i, D) for i in range(2)]
        xscr, fscr = ar(10240, D), ar(10240, D)
        ysh = ar(R4, 3072).rearrange("p (t n) -> p t n", t=TT)
        sgl = [ar(36912 + 256 * i, 256) for i in range(2)]
        hid = [ar(37424 + 256 * i, 256) for i in range(2)]
        rw_sb, rbias = ar(38448, 512), ar(38960, E_N)
        hidT = [ar(39040 + 256 * i, 256).rearrange("p (c t) -> p c t", c=2) for i in range(2)]
        lists = ar(39600, 768).bitcast(I32).rearrange("p (b e w) -> p b e w", b=3, e=E_N)
        scores = ar(40368, 192).rearrange("p (t e) -> p t e", t=TT)
        biased = ar(40560, 192).rearrange("p (t e) -> p t e", t=TT)
        m8 = ar(40752, 192).rearrange("p (t g e) -> p t g e", t=TT, g=8)
        grp, gm, gi, gif, gmask, gneg, em, ei, eif = (
            ar(40944 + 24 * i, 24).rearrange("p (t g) -> p t g", t=TT) for i in range(9))
        gi, ei = gi.bitcast(U32), ei.bitcast(U32)
        eq = ar(41160, 96).rearrange("p (t g k) -> p t g k", t=TT, g=8)
        iota = ar(41256, E_N)
        gk = ar(41320, 18).rearrange("p (t k) -> p t k", t=TT)
        wsum = ar(41338, TT)
        posx = ar(41344, 192).rearrange("p (t e) -> p t e", t=TT)
        emask = ar(41536, 192).rearrange("p (t e) -> p t e", t=TT)
        dest = ar(41728, 18).rearrange("p (t k) -> p t k", t=TT)
        desti = ar(41748, 18).bitcast(I32)
        rec = ar(41768, 72).bitcast(I32).rearrange("p (k w) -> p k w", w=4)
        flagc = ar(41840, 1)
        flagi = ar(41841, 1)[0:1, :].bitcast(I32)
        ix = [ar(41844 + 4 * i, 4).bitcast(I32) for i in range(4)]
        gx = [ar(43024 + 4 * i, 4).bitcast(I32) for i in range(4)]
        oh = ar(41872, 1152).rearrange("p (t k e) -> p t k e", t=TT, k=TOP_K)
        oht = ar(18480, 1152).rearrange("p (t k e) -> p t k e", t=TT, k=TOP_K)
        Gf = ar(0, 2 * D).rearrange("p (s n) -> p s n", s=2)
        yk = [ar(s, TOP_K * D) for s in (21552, 27696, 12288)]
        ssx, rx = sm(269, 3), sm(272, 3)

        def gate(u):
            return ix[u][:, 2:3].bitcast(F32)

        yk_d = nc.dram_tensor("expert_rows", [T * TOP_K, D], F32).ap()
        list_d = nc.dram_tensor("slot_lists", [T * E_N, 4], I32).ap()

        def cc(at, n=1):
            return col[:, at:at + n]

        win = A["w_in"].rearrange("(p c) n -> p c n", c=KC)
        wada = A["w_ada"].rearrange("(p c) n -> p c n", c=KC)
        w_chunk = [ar(chunk_at[i], KC * P * n).rearrange("p (c n) -> p c n", c=KC)
                   for i, (_, n) in enumerate(CHUNKS)]

        def by(eng, out, in0, in1):
            return eng.tensor_tensor(out.rearrange("p (b t) -> p b t", b=3), in0.rearrange("p (b t) -> p b t", b=3),
                                     in1, ALU.mult)

        block = ctx.enter_context(nc.Block())

        @block.sync
        def _(sp):
            sp.dma_start(cvec, A["cvec"]).then_inc(sem("d_cvec"), 16)

            def ada(n):
                if n >= 3:
                    sp.wait_ge(sem("ada_ps"), n - 2)
                if n >= 2:
                    sp.wait_ge(sem("mod_ev"), n - 1)
                sp.dma_start(ring[n % 3], wada[:, :, n * 512:(n + 1) * 512]).then_inc(sem(f"d_ada{n % 3}"), 16)
                sp.dma_start(adarow[0:2, (n % 2) * 1024:(n % 2 + 1) * 1024],
                             A["adarows"][n, :].partition_broadcast(2)).then_inc(sem(f"d_ada{n % 3}"), 16)

            def chunk(i):
                c0, n = CHUNKS[i]
                sp.dma_start(w_chunk[i], win[:, :, c0:c0 + n * P]).then_inc(sem(f"d_win{i}"), 16)

            ada(0)
            ada(1)
            for t in range(TT):
                sp.dma_start(xin[:, t, :], A["x"][t * P:(t + 1) * P, :]).then_inc(sem("d_x"), 16)
            sp.dma_start(const[:, :], A["c_main"]).then_inc(sem("d_const"), 16)
            sp.dma_start(col[:, :], A["cols"]).then_inc(sem("d_const"), 16)
            for n in range(2, 8):
                ada(n)
            chunk(0)
            sp.dma_start(early[:, 0:N_E], A["c_early"]).then_inc(sem("d_early"), 16)
            sp.dma_start(w2d, A["decay_w2"]).then_inc(sem("d_early"), 16)
            sp.dma_start(w2a, A["iclr_a2"]).then_inc(sem("d_early"), 16)
            sp.dma_start(g2, A["gate_g2"]).then_inc(sem("d_early"), 16)
            sp.dma_start(ck, A["cache_k"]).then_inc(sem("d_early"), 16)
            sp.dma_start(cv, A["cache_v"]).then_inc(sem("d_early"), 16)
            for i in range(1, 4):
                chunk(i)
            for n in range(8, 12):
                ada(n)
            sp.wait_ge(sem("kown"), 1)
            sp.dma_start(O["cache_k"], kown).then_inc(sem("d_out"), 16)
            sp.wait_ge(sem("z_act"), I_END)
            sp.dma_start(O["cache_v"], vown[:, 0, :]).then_inc(sem("d_out"), 16)
            sp.wait_ge(sem("zero"), 5)
            for d in range(2):
                for h in range(2):
                    sp.dma_start(SD[d][64 * h:64 * h + 64, :, 64 * h:64 * h + 64],
                                 A["state"][d, h]).then_inc(sem("d_state"), 16)
            sp.wait_ge(sem("bon_ev"), 1)
            for t in range(TT):
                sp.dma_start(res[:, t, :], A["x"][t * P:(t + 1) * P, :]).then_inc(sem("d_mb"), 16)
            for i, n in enumerate(("lnx_g", "lnx_b")):
                sp.dma_start(lnx[:, i, :], A[n].partition_broadcast(P)).then_inc(sem("d_lnx"), 16)
            for d in range(2):
                sp.wait_ge(sem("st_out"), d + 1)
                for h in range(2):
                    sp.dma_start(O["state"][d, h], stout[d][64 * h:64 * h + 64, :, 64 * h:64 * h + 64]
                                 ).then_inc(sem("d_out"), 16)
            sp.wait_ge(sem("d_out"), 16 * 6)
            sp.wait_ge(sem("sd_ps"), 2)
            wo = A["w_out"].rearrange("(c p) n -> p c n", p=P)
            sp.dma_start(woR, wo[:, 4:8, :]).then_inc(sem("d_wo"), 16)
            sp.wait_ge(sem("o_ps"), 6)
            sp.dma_start(woA, wo[:, 0:4, :]).then_inc(sem("d_wo"), 16)
            for a, sec in enumerate((2, 4, 3)):
                for s in range(2):
                    sp.dma_start(MB[:, a, s, :], mod_d[s, sec * D:(sec + 1) * D].partition_broadcast(P)
                                 ).then_inc(sem("d_mb"), 16)
            sp.wait_ge(sem("rw"), 3)
            sp.dma_start(rw_sb, A["router_w"]).then_inc(sem("d_route"), 16)
            sp.dma_start(slot13[3], A["shared13"]).then_inc(sem("d_shared"), 16)
            sp.dma_start(slotd[3], A["shared_wd"]).then_inc(sem("d_shared"), 16)
            sp.dma_start(slot13[0], A["w13"][0]).then_inc(sem("d_we0"), 16)
            sp.dma_start(slotd[0], A["wd"][0]).then_inc(sem("d_we0"), 16)
            sp.wait_ge(sem("y_ps"), TT)
            sp.dma_start(iota, A["c_iota"]).then_inc(sem("d_route"), 16)
            sp.dma_start(rec.rearrange("p k w -> p (k w)"), A["c_rec"]).then_inc(sem("d_route"), 16)
            sp.dma_start(rbias, A["router_b"].partition_broadcast(P)).then_inc(sem("d_route"), 16)
            for t in range(TT):
                sp.wait_ge(sem("h2"), t + 1)
                sp.dma_start(h2_d[t * P:(t + 1) * P, :], h2[:, t, :]).then_inc(sem("d_h2"), 16)

            def load_expert(u, e, it):
                sp.dma_start(slot13[u], A["w13"][e]).then_inc(sem(f"d_we{u}"), 16)
                sp.dma_start(slotd[u], A["wd"][e]).then_inc(sem(f"d_we{u}"), 16)

            load_expert(1, 1, 0)
            sp.wait_ge(sem("shared_ps"), TT)
            sp.wait_ge(sem("d_h2"), 48)
            sp.wait_ge(sem("d_xg0"), 16)
            load_expert(2, 2, 0)
            load_expert(3, 3, 0)
            with sp.Fori(1, NB) as it:
                for u in range(4):
                    sp.wait_ge(sem("dn_ps"), it * 4 + (u - 3))
                    load_expert(u, it * 4 + u, it)
            sp.wait_ge(sem("route"), 8)
            flag = sp.value_load(flagi[0:1, 0:1], min_val=0, max_val=1)
            with sp.If(flag > 0):
                sp.wait_ge(sem("dn_ps"), E_N)
                for b in range(2):
                    with sp.Fori(0, E_N) as e:
                        sp.dma_start(slot13[0], A["w13"][e]).then_inc(sem("d_ov"), 16)
                        sp.dma_start(slotd[0], A["wd"][e]).then_inc(sem("d_ov"), 16)
                        sp.wait_ge(sem("over"), (e + b * E_N + 1) * 11)
                        sp.sem_inc(sem("go"), 1)
            sp.wait_ge(sem("dn_ps"), E_N)
            sp.wait_ge(sem("scat"), 1)
            for t in range(TT):
                src = yk_d[t * P * TOP_K:(t + 1) * P * TOP_K, :].rearrange("(p k) n -> p (k n)", k=TOP_K)
                for hf in range(2):
                    n = slice(hf * TOP_K * D // 2, (hf + 1) * TOP_K * D // 2)
                    sp.dma_start(yk[t][:, n], src[:, n]).then_inc(sem(f"d_yk{t}{hf}"), 16)
                if t == 0:
                    for s in range(2):
                        sp.dma_start(Gf[:, s, :], mod_d[s, 5 * D:6 * D].partition_broadcast(P)
                                     ).then_inc(sem("d_gf"), 16)
            for t in range(TT):
                sp.wait_ge(sem("fin"), t + 1)
                sp.dma_start(O["y"][t * P:(t + 1) * P, :], res[:, t, :]).then_inc(sem("d_out"), 16)
            sp.wait_ge(sem("d_out"), 16 * 9)

        @block.gpsimd
        def _(pool):
            pool.memset(sm(684), 0.0).then_inc(sem("zero"), 1)

            def store_mod(n):
                pool.wait_ge(sem("mod_ev"), n + 1)
                pool.dma_start(mod_d[:, n * 512:(n + 1) * 512],
                               modrow[0:2, (n % 2) * 512:(n % 2 + 1) * 512]).then_inc(sem(f"mod_st{n % 2}"), 16)

            for n in range(4):
                store_mod(n)
            pool.wait_ge(sem("mod_st0"), 32)
            pool.wait_ge(sem("mod_st1"), 32)
            for a in range(2):
                for s in range(2):
                    pool.dma_start(mcol[:, a, s, :], mod_d[s, a * D:(a + 1) * D].rearrange("(p c) -> p c", c=KC)
                                   ).then_inc(sem("d_mcol"), 16)
            for n in range(4, 12):
                store_mod(n)
            pool.wait_ge(sem("ei"), 1)
            pool.wait_ge(sem("hb_ev"), 9)
            pool.wait_ge(sem("rope"), 6)
            for dj in range(8):
                ins = pool.tensor_tensor(bM[:, dj, :], aic[:, dj, :], kkb[:, dj % 4, :], ALU.mult)
            ins.then_inc(sem("zero"), 1)
            pool.wait_ge(sem("zero"), 2)
            for d in range(2):
                for j in range(4):
                    dj = 4 * d + j
                    e, iv = Ebuf[:, dj], Ibuf[:, dj]
                    by(pool, bM[:, dj, :], bM[:, dj, :], iv[:, :, 1:P + 1] if d == 0 else e[:, :, 0:P])
                    by(pool, aM[:, dj, :], kkb[:, j, :], e[:, :, 0:P] if d == 0 else iv[:, :, 1:P + 1])
                    ins = by(pool, rM[:, dj, :], zs[:, j, :], e[:, :, 1:P + 1] if d == 0 else iv[:, :, 0:P])
            ins.then_inc(sem("zero"), 1)
            pool.wait_ge(sem("prep"), 4)
            pool.wait_ge(sem("bon_ev"), 1)
            pool.wait_ge(sem("zero"), 3)
            for d in range(2):
                pool.memset(SD[d], 0.0).then_inc(sem("zero"), 1)
            pool.wait_ge(sem("mod_st0"), 96)
            pool.wait_ge(sem("mod_st1"), 96)
            pool.dma_start(list_d, A["c_list"]).then_inc(sem("d_list"), 16)
            pool.wait_ge(sem("sh_up"), 1)
            pool.tensor_tensor(hid[0], sgl[0], sgl[1], ALU.mult).then_inc(sem("sh_hid"), 1)
            pool.wait_ge(sem("route"), 5)
            pool.wait_ge(sem("d_list"), 16)
            for k in range(TT * TOP_K):
                pool.indirect_dma_start(out=list_d, out_offset=bass.IndirectOffsetOnAxis(ap=desti[:, k:k + 1], axis=0),
                                        in_=rec[:, k, :], in_offset=None, bounds_check=T * E_N - 1,
                                        oob_is_err=False).then_inc(sem("d_list"), 16)
            pool.wait_ge(sem("h2"), TT)
            pool.wait_ge(sem("route"), 5)
            for b in range(4):
                pool.memset(xg[b], 0.0).then_inc(sem("zero"), 1)
            pool.wait_ge(sem("d_list"), 16 * (TT * TOP_K + 1))
            pool.dma_start(lists, list_d.rearrange("(b p e) w -> p b e w", b=3, p=P)).then_inc(sem("d_list"), 16)
            pool.wait_ge(sem("d_list"), 16 * (TT * TOP_K + 2))
            pool.wait_ge(sem("d_h2"), 48)
            pool.wait_ge(sem("zero"), 9)
            n_ix = sem("ix")
            last_token, last_row = pool.to_reg(T - 1), pool.to_reg(T * TOP_K - 1)

            def gather(u, e, first):
                if not first:
                    pool.wait_ge(sem("xt2"), e - 3)
                    pool.sem_inc(sem("go"), 1)
                pool.tensor_copy(gx[u], lists[:, 0, bass.ds(e, 1), :].rearrange("p e w -> p (e w)")).then_inc(n_ix, 1)
                pool.wait_ge(sem("d_h2"), 48)
                pool.wait_ge(n_ix, e + 1 if isinstance(e, int) and e < 3 else e * 2 - 1)
                if not first:
                    pool.wait_ge(sem("xt2"), e - 3)
                pool.sem_inc(sem("go"), 1)
                pool.indirect_dma_start(out=xg[u], out_offset=None, in_=h2_d,
                                        in_offset=bass.IndirectOffsetOnAxis(ap=gx[u][:, 1:2], axis=0),
                                        bounds_check=last_token, oob_is_err=False).then_inc(sem(f"d_xg{u}"), 16)

            def rows(u, e, it, first):
                if not first:
                    pool.wait_ge(sem(f"d_sc{u}"), 16 * it)
                    pool.sem_inc(sem("go"), 1)
                pool.tensor_copy(ix[u], lists[:, 0, bass.ds(e, 1), :].rearrange("p e w -> p (e w)")).then_inc(n_ix, 1)

            def scatter(u, e):
                pool.wait_ge(sem("d_list"), 16 * (TT * TOP_K + 2))
                pool.wait_ge(n_ix, e * 2 + 4)
                pool.wait_ge(sem("yv"), e + 1)
                pool.wait_ge(sem("ya"), e + 1)
                pool.sem_inc(sem("go"), 1)
                pool.indirect_dma_start(out=yk_d, out_offset=bass.IndirectOffsetOnAxis(ap=ix[u][:, 0:1], axis=0),
                                        in_=yb[u % 2], in_offset=None, bounds_check=last_row,
                                        oob_is_err=False).then_inc(sem(f"d_sc{u}"), 16)

            for u in range(3):
                gather(u, u, True)
            rows(0, 0, 0, True)
            for u in range(4):
                gather((u + 3) % 4, u + 3, u == 0)
                rows((u + 1) % 4, u + 1, 1, u < 3)
                scatter(u, u)
            with pool.Fori(1, NB - 1) as it:
                for u in range(4):
                    gather((u + 3) % 4, it * 4 + (u + 3), False)
                    rows((u + 1) % 4, it * 4 + (u + 1), it + (1 if u == 3 else 0), False)
                    scatter(u, it * 4 + u)
            for u in range(4):
                if u == 0:
                    gather(3, E_N - 1, False)
                else:
                    pool.wait_ge(n_ix, 2 * (E_N - 4 + u) + 4)
                    pool.sem_inc(n_ix, 1)
                if u < 3:
                    rows(u + 1, E_N - 3 + u, NB - 1, False)
                scatter(u, E_N - 4 + u)
            for u in range(4):
                pool.wait_ge(sem(f"d_sc{u}"), 16 * NB)
            pool.wait_ge(sem("route"), 8)
            flag = pool.value_load(flagi[0:1, 0:1], min_val=0, max_val=1)
            with pool.If(flag > 0):
                for b in range(2):
                    with pool.Fori(0, E_N) as e:
                        n = e + b * E_N
                        pool.tensor_copy(ix[0], lists[:, b + 1, bass.ds(e, 1), :].rearrange("p e w -> p (e w)")
                                         ).then_inc(sem("over"), 1)
                        pool.wait_ge(sem("d_h2"), 48)
                        pool.wait_ge(sem("over"), n * 11 + 1)
                        pool.sem_inc(sem("go"), 1)
                        pool.indirect_dma_start(out=xg[0], out_offset=None, in_=h2_d,
                                                in_offset=bass.IndirectOffsetOnAxis(ap=ix[0][:, 1:2], axis=0),
                                                bounds_check=last_token, oob_is_err=False).then_inc(sem("d_ovx"), 16)
                        pool.wait_ge(sem("d_list"), 16 * (TT * TOP_K + 2))
                        pool.wait_ge(sem("over"), n * 11 + 10)
                        pool.sem_inc(sem("go"), 1)
                        pool.indirect_dma_start(out=yk_d, out_offset=bass.IndirectOffsetOnAxis(ap=ix[0][:, 0:1], axis=0),
                                                in_=yb[0], in_offset=None, bounds_check=last_row,
                                                oob_is_err=False).then_inc(sem("d_ovx"), 16)
                        pool.wait_ge(sem("d_ovx"), (n + 1) * 32)
                        pool.sem_inc(sem("over"), 1)
            pool.sem_inc(sem("scat"), 1)

        @block.scalar
        def _(act):
            n_own = [0]

            def own(ins):
                n_own[0] += 1
                ins.then_inc(sem("act_own"), 1)
                act.wait_ge(sem("act_own"), n_own[0])

            act.wait_ge(sem("d_cvec"), 16)
            act.activation(csil.rearrange("p c s -> p (c s)"), cvec, ACT.Silu).then_inc(sem("csil"), 1)
            act.wait_ge(sem("d_x"), 48)
            for t in range(TT):
                if t:
                    act.wait_ge(sem("ss"), t)
                act.activation(ps[:, 6:8, :].rearrange("p a n -> p (a n)"), xin[:, t, :], ACT.Square,
                               accum_out=ss[:, t:t + 1]).then_inc(sem("ss"), 1)
            act.wait_ge(sem("ss"), 3)
            act.wait_ge(sem("d_const"), 32)
            act.activation(rstd, ss, ACT.Sqrt, scale=1.0 / D, bias=cst("eps")).then_inc(sem("rt"), 1)
            act.wait_ge(sem("acol"), 1)
            for t in range(TT):
                act.wait_ge(sem("xt_ps"), 2 * t + 2)
                for c in range(4, 8):
                    ins = act.activation(hT[:, c, t * P:(t + 1) * P], ps[:, 3 + 2 * t, (c - 4) * P:(c - 3) * P],
                                         ACT.Identity, scale=Acol[:, min(t, 1), c:c + 1],
                                         bias=mcol[:, 0, min(t, 1), c:c + 1])
                ins.then_inc(sem("ht_act"), 1)

            def z(i):
                act.wait_ge(sem("z_ps"), i + 1)
                b = ps[:, 2 + i % 6, 0:T]
                if i < I_DI:
                    j = Z_ORDER[i]
                    act.wait_ge(sem("c1"), 1)
                    ins = act.activation(zs[:, j, :], b, ACT.Copy, scale=c1[:, j:j + 1])
                elif i < I_ATT:
                    a, dj = divmod(i - I_DI, 8)
                    ins = act.activation((wdec, aic)[a][:, dj, :], b, ACT.Sigmoid, bias=cc((C_W0, C_A0)[a] + dj))
                elif i < I_V:
                    ins = act.activation(raw[:, i - I_ATT, :], b, ACT.Copy)
                else:
                    ins = act.activation(vown.rearrange("p a t -> p (a t)"), b, ACT.Copy)
                ins.then_inc(sem("z_act"), 1)

            for i in range(10):
                z(i)
            act.wait_ge(sem("z_dve"), 5)
            act.activation(zs[:, 12, :], zs[:, 12, :], ACT.Tanh).then_inc(sem("lowr"), 1)
            act.activation(zs[:, 14, :], zs[:, 14, :], ACT.Sigmoid).then_inc(sem("lowr"), 1)
            for i in range(10, I_ATT):
                z(i)
            act.wait_ge(sem("z_act"), I_ATT)
            act.activation(wdec.rearrange("p a t -> p (a t)"), wdec.rearrange("p a t -> p (a t)"), ACT.Exp,
                           scale=-DECAY_SCALE).then_inc(sem("decay"), 1)
            for i in range(I_ATT, I_END):
                z(i)
            act.wait_ge(sem("z_act"), I_END)
            act.wait_ge(sem("z_dve"), NZ)
            for j in range(5):
                act.activation(sq9[:, j, :], raw[:, j, :], ACT.Square).then_inc(sem("sq"), 1)
            for j in range(4):
                act.activation(sq9[:, 5 + j, :], zs[:, 4 + j, :], ACT.Square, scale=cc(C_KK + j)
                               ).then_inc(sem("sq"), 1)
            act.wait_ge(sem("nrm"), 1)
            act.activation(rs18, ps[0:18, 0, 0:T], ACT.Sqrt, scale=cst("nscale")[0:18, :],
                           bias=cst("nbias")[0:18, :]).then_inc(sem("nrm"), 1)
            act.wait_ge(sem("ko_ps"), 1)
            act.activation(kown, ps[:, 7, 0:P], ACT.Copy).then_inc(sem("kown"), 1)
            act.activation(kall[:, P:2 * P], ps[:, 7, P:2 * P], ACT.Copy).then_inc(sem("kown"), 1)
            act.wait_ge(sem("rope"), 6)
            for t in range(TT):
                act.wait_ge(sem("vt_ps"), t + 1)
                act.activation(Vtok[:, t, :], ps[:, 4 + t, :], ACT.Copy).then_inc(sem("vt_ev"), 1)
            for kv in range(2):
                act.wait_ge(sem("dup_ps"), kv + 1)
                act.activation(kdup[:, kv, :], ps[:, 2 + kv, :], ACT.Copy).then_inc(sem("dup_ev"), 1)
            for t in range(TT):
                act.wait_ge(sem("vt_ps"), TT + t + 1)
                act.activation(gtok[:, t, :], ps[:, 4 + t, :], ACT.Copy).then_inc(sem("vt_ev"), 1)
            for g in range(6):
                qt = g // 2
                nk = 1 if qt == 0 else 3
                for i in range(4):
                    act.wait_ge(sem("mx"), 4 * g + i + 1)
                    if g:
                        act.wait_ge(sem("pt_ps"), g)
                    act.activation(Pb[:, i, 0:nk * P], ps[:, i, 0:nk * P], ACT.Exp, bias=nmx[:, i:i + 1],
                                   accum_out=rsum[:, i:i + 1]).then_inc(sem("ex"), 1)
                act.wait_ge(sem("pt_ps"), g + 1)
                if g:
                    act.wait_ge(sem("pv_ps"), g)
                for kt in range(nk):
                    act.activation(PTb[:, kt, :], ps[:, 4 + kt, :], ACT.Copy).then_inc(sem("pt_ev"), 1)
            for p in range(3):
                for d in range(2):
                    for par in range(2):
                        act.wait_ge(sem("lt_ps"), 4 * p + 2 * d + par + 1)
                        act.activation(LT[d][:, 4 * par:4 * par + 4, :].rearrange("p u t -> p (u t)"),
                                       ps[:, par, :], ACT.Copy).then_inc(sem("lt_ev"), 1)
                for d in range(2):
                    for par in range(2):
                        act.wait_ge(sem("t_ps"), 28 * p + 2 * d + par + 1)
                        act.activation(X[d][:, 4 * par:4 * par + 4, :].rearrange("p u t -> p (u t)"),
                                       ps[:, 4 * d + 2 + par, :], ACT.Copy).then_inc(sem("t_ev"), 1)
                if p == 1:
                    for d in range(2):
                        act.wait_ge(sem("so_ps"), d + 1)
                        act.activation(stout[d].rearrange("p j t -> p (j t)"), ps[:, 4 * d + 1, :], ACT.Copy
                                       ).then_inc(sem("st_out"), 1)
                for l in range(len(LEVELS)):
                    for d in range(2):
                        for par in range(2):
                            act.wait_ge(sem("t_ps"), 28 * p + 4 * (l + 1) + 2 * d + par + 1)
                            act.activation(Y[d][:, 4 * par:4 * par + 4, :].rearrange("p u t -> p (u t)"),
                                           ps[:, 4 * d + 2 + par, :], ACT.Copy).then_inc(sem("t_ev"), 1)
                for d in range(2):
                    act.wait_ge(sem("w_ps"), 2 * p + d + 1)
                    act.activation(Ws[d], ps[:, d, :], ACT.Copy, scale=-1.0).then_inc(sem("w_ev"), 1)
                if p < 2:
                    for d in range(2):
                        for h in range(2):
                            act.wait_ge(sem("bk_ps"), 4 * p + 2 * d + h + 1)
                            if p:
                                act.wait_ge(sem("s_ps"), 2 * (p - 1) + d + 1)
                            act.activation(bktok[d][:, 4 * h:4 * h + 4, :].rearrange("p a t -> p (a t)"),
                                           ps[:, 6 - 2 * d + h, :], ACT.Copy).then_inc(sem("bk_ev"), 1)
            for t in range(TT):
                act.wait_ge(sem("gn"), 4 * t + 1)
                act.activation(wtmp, Obuf[:, t, :], ACT.Square).then_inc(sem("gn"), 1)
                act.wait_ge(sem("gn"), 4 * t + 3)
                act.activation(gst[:, 8:16], gst[:, 0:8], ACT.Sqrt, scale=1.0 / 64, bias=cst("gneps")
                               ).then_inc(sem("gn"), 1)
            for t in range(TT):
                act.wait_ge(sem("rw_ps"), t + 1)
                act.activation(rwT[:, :, t * P:(t + 1) * P], ps[:, 6 + t % 2, :].rearrange("p (a t) -> p a t", a=4),
                               ACT.Copy).then_inc(sem("rw_ev"), 1)
            for t in range(TT):
                act.wait_ge(sem("y_ps"), t + 1)
                for hf in range(2):
                    if t + hf:
                        act.wait_ge(sem("ysq"), 2 * t + hf)
                    act.activation(wtmp, ps[:, 2 * t + hf, :], ACT.Square,
                                   accum_out=ssh[:, 2 * t + hf:2 * t + hf + 1]).then_inc(sem("ysq"), 1)
                act.wait_ge(sem("yss"), t + 1)
                act.activation(ry[:, t:t + 1], ssy[:, t:t + 1], ACT.Sqrt, scale=1.0 / D, bias=cst("eps")
                               ).then_inc(sem("yrt"), 1)
                act.wait_ge(sem("x1"), t + 1)
                if t:
                    act.wait_ge(sem("xsq"), t)
                act.activation(xscr, res[:, t, :], ACT.Square, accum_out=ssx[:, t:t + 1]).then_inc(sem("xsq"), 1)
                act.wait_ge(sem("xsq"), t + 1)
                act.activation(rx[:, t:t + 1], ssx[:, t:t + 1], ACT.Sqrt, scale=1.0 / D, bias=cst("eps")
                               ).then_inc(sem("xrt"), 1)
            for t in range(TT):
                for hf in range(2):
                    act.wait_ge(sem("ht2_ps"), 2 * t + hf + 1)
                    act.activation(h2T[:, 4 * hf:4 * hf + 4, t * P:(t + 1) * P],
                                   ps[:, 6 + hf, :].rearrange("p (c t) -> p c t", c=4), ACT.Copy
                                   ).then_inc(sem("ht2_ev"), 1)
            act.wait_ge(sem("route"), 1)
            act.activation(scores.rearrange("p t e -> p (t e)"), ps[:, 0, 0:TT * E_N], ACT.Sigmoid
                           ).then_inc(sem("route"), 1)
            for t in range(TT):
                act.wait_ge(sem("sh_gu"), t + 1)
                if t:
                    act.wait_ge(sem("sh_hid"), t)
                act.activation(sgl[0], ps[:, 2, 0:FF], ACT.Silu)
                act.activation(sgl[1], ps[:, 2, FF:2 * FF], ACT.Copy).then_inc(sem("sh_up"), 1)
                act.wait_ge(sem("sh_at"), t + 1)
                if t:
                    act.wait_ge(sem("shared_ps"), t)
                act.activation(hidT[0].rearrange("p c t -> p (c t)"), ps[:, 3, 0:2 * P], ACT.Copy
                               ).then_inc(sem("sh_att"), 1)
                act.wait_ge(sem("shared_ps"), t + 1)
                act.activation(ysh[:, t, :], ps[:, 4:6, :].rearrange("p a n -> p (a n)"), ACT.Copy
                               ).then_inc(sem("sh_y"), 1)

            def silu(u, e):
                act.wait_ge(sem("gu_ps"), e + 1)
                if not (isinstance(e, int) and e < 2):
                    act.wait_ge(sem("hid"), e - 1)
                act.activation(sgl[u % 2], ps[:, 2 + u % 2, 0:FF], ACT.Silu).then_inc(sem("sg"), 1)

            def tokens_t(u, e):
                act.wait_ge(sem("xt2"), e + 1)
                if not (isinstance(e, int) and e < 2):
                    act.wait_ge(sem("gu_ps"), e - 1)
                act.activation(xgT[u % 2][:, 4:8, :].rearrange("p c t -> p (c t)"), ps[:, 1, :], ACT.Copy
                               ).then_inc(sem("xta"), 1)

            def out_half(u, e, it):
                act.wait_ge(sem("dn_ps"), e + 1)
                act.wait_ge(sem("ix"), e * 2 + 4)
                if not (isinstance(e, int) and e < 2):
                    act.wait_ge(sem(f"d_sc{(u + 2) % 4}"), 16 * (it + (1 if u >= 2 else 0)))
                act.activation(yb[u % 2][:, 512:1024], ps[:, 6, :], ACT.Copy, scale=gate(u)).then_inc(sem("ya"), 1)

            def hidden_t(u, e):
                act.wait_ge(sem("at2"), e + 1)
                if not (isinstance(e, int) and e < 2):
                    act.wait_ge(sem("dn_ps"), e - 1)
                act.activation(hidT[u % 2].rearrange("p c t -> p (c t)"), ps[:, 4, 0:2 * P], ACT.Copy
                               ).then_inc(sem("hta"), 1)

            def expert(u, e, it, last=False):
                silu(u, e)
                if not last:
                    tokens_t((u + 1) % 4, e + 1)
                if not (isinstance(e, int) and e == 0):
                    out_half((u + 3) % 4, e - 1, it - (1 if u == 0 else 0))
                hidden_t(u, e)

            tokens_t(0, 0)
            for u in range(4):
                expert(u, u, 0)
            with act.Fori(1, NB - 1) as it:
                for u in range(4):
                    expert(u, it * 4 + u, it)
            for u in range(4):
                expert(u, E_N - 4 + u, NB - 1, last=u == 3)
            out_half(3, E_N - 1, NB - 1)
            act.wait_ge(sem("route"), 8)
            flag = act.value_load(flagi[0:1, 0:1], min_val=0, max_val=1)
            with act.If(flag > 0):
                for b in range(2):
                    with act.Fori(0, E_N) as e:
                        n = e + b * E_N
                        act.wait_ge(sem("over"), n * 11 + 2)
                        act.activation(xgT[0].rearrange("p c t -> p (c t)"),
                                       ps[:, 0:2, :].rearrange("p a n -> p (a n)"), ACT.Copy).then_inc(sem("over"), 1)
                        act.wait_ge(sem("over"), n * 11 + 4)
                        act.activation(sgl[0], ps[:, 2, 0:FF], ACT.Silu).then_inc(sem("over"), 1)
                        act.wait_ge(sem("over"), n * 11 + 7)
                        act.activation(hidT[0].rearrange("p c t -> p (c t)"), ps[:, 4, 0:2 * P], ACT.Copy
                                       ).then_inc(sem("over"), 1)
                        act.wait_ge(sem("over"), n * 11 + 9)
                        act.activation(yb[0], ps[:, 5:7, :].rearrange("p a n -> p (a n)"), ACT.Copy, scale=gate(0)
                                       ).then_inc(sem("over"), 1)
            for t in range(TT):
                act.wait_ge(sem("moe"), t + 1)
                act.wait_ge(sem("xsq"), TT + t)
                act.activation(fscr, ysh[:, t, :], ACT.Square, accum_out=ssx[:, t:t + 1]).then_inc(sem("xsq"), 1)
                act.wait_ge(sem("xsq"), TT + t + 1)
                act.activation(rx[:, t:t + 1], ssx[:, t:t + 1], ACT.Sqrt, scale=1.0 / D, bias=cst("eps")
                               ).then_inc(sem("xrt"), 1)

        @block.vector
        def _(dve):
            n_own = [0]

            def own(ins):
                n_own[0] += 1
                ins.then_inc(sem("dve_own"), 1)
                dve.wait_ge(sem("dve_own"), n_own[0])

            told = {}

            def tell(ins, name):
                told[name] = told.get(name, 0) + 1
                ins.then_inc(sem(name), 1)
                dve.wait_ge(sem(name), told[name])

            def mod(n):
                sec = n // 2
                dve.wait_ge(sem("ada_ps"), n + 1)
                dve.wait_ge(sem(f"d_ada{n % 3}"), 32 * (n // 3 + 1))
                if n >= 2:
                    dve.wait_ge(sem(f"mod_st{n % 2}"), 16 * (n // 2))
                out = modrow[0:2, (n % 2) * 512:(n % 2 + 1) * 512]
                b = adarow[0:2, (n % 2) * 1024:(n % 2) * 1024 + 512]
                g = adarow[0:2, (n % 2) * 1024 + 512:(n % 2) * 1024 + 1024]
                if sec in (0, 1, 3):
                    tell(dve.tensor_tensor(out, ps[0:2, n % 2, :], b, ALU.add), "mod_ev")
                else:
                    own(dve.tensor_tensor(out, ps[0:2, n % 2, :], b, ALU.add))
                    tell(dve.scalar_tensor_tensor(out=out, in0=out, scalar=1.0 if sec == 4 else 0.0, in1=g,
                                                  op0=ALU.add, op1=ALU.mult), "mod_ev")

            mod(0)
            mod(1)
            dve.wait_ge(sem("rt"), 1)
            own(dve.reciprocal(rstd, rstd))
            for t in range(TT):
                tell(dve.tensor_scalar(xin[:, t, :], xin[:, t, :], rstd[:, t:t + 1], None, ALU.mult), "xn")
            own(dve.tensor_tensor(c1, cc(C_MP, 15), cc(C_MN, 15), ALU.add))
            tell(dve.tensor_scalar(c1, c1, -1.0, 1.0, ALU.mult, ALU.add), "c1")
            own(dve.tensor_scalar(ka1, cc(C_KA, 4), -1.0, 1.0, ALU.mult, ALU.add))
            for n in range(2, 8):
                mod(n)
            dve.wait_ge(sem("d_mcol"), 64)
            for s in range(2):
                ins = dve.scalar_tensor_tensor(out=Acol[:, s, :], in0=mcol[:, 1, s, :], scalar=1.0,
                                               in1=cc(C_GPRE, 8), op0=ALU.add, op1=ALU.mult)
            tell(ins, "acol")
            for t in range(TT):
                dve.wait_ge(sem("xt_ps"), 2 * t + 1)
                for c in range(4):
                    ins = dve.tensor_scalar(hT[:, c, t * P:(t + 1) * P], ps[:, 2 + 2 * t, c * P:(c + 1) * P],
                                            Acol[:, min(t, 1), c:c + 1], mcol[:, 0, min(t, 1), c:c + 1],
                                            ALU.mult, ALU.add)
                ins.then_inc(sem("ht_dve"), 1)

            def shift(i):
                j = Z_ORDER[i]
                b = ps[:, 2 + i % 6, :]
                dve.wait_ge(sem("z_act"), i + 1)
                for m, off in ((C_MP, -1), (C_MN, 1)):
                    for lo, hi in ((0, P), (P, T)):
                        a, e = (lo + 1, hi) if off < 0 else (lo, hi - 1)
                        ins = dve.scalar_tensor_tensor(out=zs[:, j, a:e], in0=b[:, a + off:e + off],
                                                       scalar=cc(m + j), in1=zs[:, j, a:e],
                                                       op0=ALU.mult, op1=ALU.add)
                        if (m, lo) == (C_MN, P):
                            tell(ins, "z_dve")
                        else:
                            own(ins)

            for i in range(15):
                shift(i)
            mod(8)
            mod(9)
            dve.wait_ge(sem("decay"), 1)
            dve.wait_ge(sem("zero"), 1)
            for d in range(2):
                for j in range(4):
                    dj = 4 * d + j
                    w, e, iv = wdec[:, dj, :], Ebuf[:, dj], Ibuf[:, dj]
                    own(dve.memset(e[:, :, 0:1], 1.0))
                    for b in range(3):
                        own(dve.tensor_tensor_scan(e[:, b, 1:P + 1], w[:, b * P:(b + 1) * P], zero, 1.0,
                                                   ALU.mult, ALU.add))
                    own(dve.reciprocal(rc[:, 3 * dj:3 * dj + 3], e[:, :, 64]))
                    own(dve.tensor_tensor(e, e, wide(rc[:, 3 * dj:3 * dj + 3], P + 1), ALU.mult))
                    own(dve.reciprocal(iv, e))
                    first, last = (iv[:, :, 0], e[:, :, P]) if d == 0 else (e[:, :, P], iv[:, :, 0])
                    own(dve.tensor_copy(scS[:, 3 * dj:3 * dj + 3], first))
                    own(dve.tensor_copy(scE[:, 3 * dj:3 * dj + 3], last))
            dve.sem_inc(sem("ei"), 1)
            mod(10)
            mod(11)

            dve.wait_ge(sem("nrm"), 2)
            dve.reciprocal(rs18, rs18).then_inc(sem("nrm"), 1)
            for j in range(9):
                dve.wait_ge(sem("hb_ps"), j + 1)
                b = ps[:, 2 + j % 6, 0:T]
                if j < 5:
                    ins = dve.scalar_tensor_tensor(out=raw[:, j, :], in0=raw[:, j, :],
                                                   scalar=cc(C_QG if j < 4 else C_KG), in1=b,
                                                   op0=ALU.mult, op1=ALU.mult)
                else:
                    ins = dve.scalar_tensor_tensor(out=kkb[:, j - 5, :], in0=zs[:, j - 1, :],
                                                   scalar=cc(C_KK + j - 5), in1=b, op0=ALU.mult, op1=ALU.mult)
                tell(ins, "hb_ev")
            for j in range(5):
                dve.wait_ge(sem("rp_ps"), j + 1)
                tell(dve.tensor_tensor(sq9[:, j, :], ps[:, j % 2, 0:T], erl("sin"), ALU.mult), "rp_ev")
                if j < 4:
                    own(dve.tensor_tensor(qr[:, j, :], raw[:, j, :], erl("cos"), ALU.mult))
                    tell(dve.tensor_tensor(qr[:, j, :], qr[:, j, :], sq9[:, j, :], ALU.add), "rope")
                else:
                    own(dve.tensor_tensor(sq9[:, 5, :], raw[:, j, :], erl("cos"), ALU.mult))
                    tell(dve.tensor_tensor(kall[:, 0:P], sq9[:, 5, 0:P], sq9[:, j, 0:P], ALU.add), "rope")
                    tell(dve.tensor_tensor(kall[:, 2 * P:4 * P], sq9[:, 5, P:T], sq9[:, j, P:T], ALU.add), "rope")

            def prep(j):
                for d in range(2):
                    dj = 4 * d + j
                    a, e, iv = aic[:, dj, :], Ebuf[:, dj], Ibuf[:, dj]
                    own(dve.tensor_scalar(tmp[d], a, cc(C_KA + j), ka1[:, j:j + 1], ALU.mult, ALU.add))
                    own(dve.tensor_tensor(tmp[d], tmp[d], zs[:, 4 + j, :], ALU.mult))
                    e0, i1 = e[:, :, 0:P], iv[:, :, 1:P + 1]
                    own(by(dve, kM[:, dj, :], tmp[d], i1 if d == 0 else e0))
                own(dve.tensor_tensor(tmp[0], tmp[0], tmp[1], ALU.add))
                tell(dve.scalar_tensor_tensor(out=zs[:, 4 + j, :], in0=tmp[0], scalar=cc(C_RK + j),
                                              in1=zs[:, j, :], op0=ALU.mult, op1=ALU.mult), "prep")

            for g in range(6):
                qt, kv = divmod(g, 2)
                nk = 1 if qt == 0 else 3
                for i in range(4):
                    dve.wait_ge(sem("sc_ps"), 4 * g + i + 1)
                    if g:
                        dve.wait_ge(sem("ex"), 4 * g)
                    tell(dve.tensor_reduce(nmx[:, i:i + 1], ps[:, i, 0:nk * P], AX.X, ALU.max, negate=True), "mx")
                for i in range(4):
                    dve.wait_ge(sem("ex"), 4 * g + i + 1)
                    own(dve.reciprocal(rsum[:, i:i + 1], rsum[:, i:i + 1]))
                    tell(dve.tensor_scalar(Pb[:, i, 0:nk * P], Pb[:, i, 0:nk * P], rsum[:, i:i + 1], None,
                                           ALU.mult), "pn")
                if g < 4:
                    prep(g)
                dve.wait_ge(sem("pv_ps"), g + 1)
                tell(dve.tensor_copy(attnT[:, 2 * kv:2 * kv + 2, qt * P:(qt + 1) * P],
                                     ps[:, 7, 0:2 * P].rearrange("p (a t) -> p a t", a=2)), "at_ev")

            for p in range(3):
                for d in range(2):
                    m = rep(cst(f"st{d}"), 4), rep(cst(f"in{d}"), 4), rep(cst(f"in{d}"), 4)
                    for par in range(2):
                        dve.wait_ge(sem("lt_ev"), 4 * p + 2 * d + par + 1)
                        y = Y[d][:, 4 * par:4 * par + 4, :]
                        own(dve.tensor_tensor(y, LT[d][:, 4 * par:4 * par + 4, :], rep(cst(f"nm{d}"), 4), ALU.mult))
                        tell(dve.tensor_tensor(y, y, rep(cst("ident"), 4), ALU.add), "y2")
                    for k, buf in enumerate((MT, RB, RK)):
                        for par in range(2):
                            dve.wait_ge(sem("m_ps"), 12 * p + 6 * d + 2 * k + par + 1)
                            tell(dve.tensor_tensor(buf[d][:, 4 * par:4 * par + 4, :],
                                                   ps[:, 2 + 2 * k + par, :].rearrange("p (u t) -> p u t", u=4),
                                                   m[k], ALU.mult), "m_ev")
                if p == 1:
                    dve.wait_ge(sem("bon_ps"), 1)
                    tell(dve.tensor_copy(bon.rearrange("p t h -> p (t h)"), ps[:, 0, 0:24]), "bon_ev")
                for l, s in enumerate(LEVELS):
                    for d in range(2):
                        dve.wait_ge(sem("h_ps"), 12 * p + 2 * l + d + 1)
                        tell(dve.tensor_tensor(Hs[d], ps[:, 4 * d, :].rearrange("p (u t) -> p u t", u=8),
                                               rep(cst(f"hm{d}")[:, 64 * l:64 * l + 64], 8), ALU.mult), "h_ev")
                    for d in range(2):
                        dve.wait_ge(sem("zz_ps"), 12 * p + 2 * l + d + 1)
                        xs = X[d].rearrange("p u (n a s) -> p u n a s", a=2, s=s)[:, :, :, d, :]
                        z4 = ps[:, 4 * d + 1, :].rearrange("p (u n s) -> p u n s", u=8, s=s)
                        tell(dve.tensor_tensor(xs, xs, z4, ALU.subtract), "x_ev")
                if p == 1:
                    for d in range(2):
                        dve.wait_ge(sem("sd_ps"), d + 1)
                        for j in range(4):
                            blk = BLOCKS[d][p]
                            k = 3 * (4 * d + j) + blk
                            ins = dve.tensor_scalar(Sp[d][:, j, :], ps[:, 6 + d, j * P:(j + 1) * P],
                                                    scS[:, k:k + 1], None, ALU.mult)
                        tell(ins, "sp")
                for d in range(2):
                    dve.wait_ge(sem("u_ps"), 2 * p + d + 1)
                    tell(dve.tensor_copy(Us[d], ps[:, 2 + d, :]), "u_ev")
                for d in range(2):
                    blk = BLOCKS[d][p]
                    dve.wait_ge(sem("o_ps"), 2 * p + d + 1)
                    first = (p, d) in ((0, 0), (1, 0), (1, 1))
                    if first:
                        tell(dve.tensor_copy(Obuf[:, blk, :], ps[:, d, :]), "o_ev")
                    else:
                        tell(dve.tensor_tensor(Obuf[:, blk, :], Obuf[:, blk, :], ps[:, d, :], ALU.add), "o_ev")
                if p < 2:
                    for d in range(2):
                        blk = BLOCKS[d][p]
                        dve.wait_ge(sem("s_ps"), 2 * p + d + 1)
                        sps = ps[:, 6 + d, :].rearrange("p (j t) -> p j t", j=4)
                        if p == 0:
                            src = sps
                        else:
                            own(dve.tensor_tensor(Sp[d], sps, Sp[d], ALU.add))
                            src = Sp[d]
                        for j in range(4):
                            k = 3 * (4 * d + j) + blk
                            ins = dve.scalar_tensor_tensor(out=Sp[d][:, j, :], in0=src[:, j, :],
                                                           scalar=scE[:, k:k + 1], in1=cst("blk"),
                                                           op0=ALU.mult, op1=ALU.mult)
                            own(ins) if (p, j) != (0, 3) else tell(ins, "s_ev")
                        if p == 1:
                            for j in range(4):
                                k = 3 * (4 * d + j) + BLOCKS[d][2]
                                ins = dve.tensor_scalar(Sp[d][:, j, :], Sp[d][:, j, :], scS[:, k:k + 1], None,
                                                        ALU.mult)
                                own(ins) if j < 3 else tell(ins, "s_ev")

            dve.wait_ge(sem("d_lnx"), 32)
            dve.wait_ge(sem("vt_ev"), 2 * TT)
            for t in range(TT):
                o = Obuf[:, t, :].rearrange("p (h v) -> p h v", h=8)
                own(dve.tensor_reduce(gst[:, 0:8], o, AX.X, ALU.add))
                own(dve.tensor_scalar(gst[:, 0:8], gst[:, 0:8], 1.0 / 64, None, ALU.mult))
                dve.tensor_tensor(o, o, wide(gst[:, 0:8], 64), ALU.subtract).then_inc(sem("gn"), 1)
                dve.wait_ge(sem("gn"), 4 * t + 2)
                dve.tensor_reduce(gst[:, 0:8], wtmp.rearrange("p (h v) -> p h v", h=8), AX.X, ALU.add
                                  ).then_inc(sem("gn"), 1)
                dve.wait_ge(sem("gn"), 4 * t + 4)
                own(dve.reciprocal(gst[:, 16:24], gst[:, 8:16]))
                own(dve.tensor_tensor(o, o, wide(gst[:, 16:24], 64), ALU.mult))
                own(dve.tensor_tensor(Obuf[:, t, :], Obuf[:, t, :], lnx[:, 0, :], ALU.mult))
                own(dve.tensor_tensor(Obuf[:, t, :], Obuf[:, t, :], lnx[:, 1, :], ALU.add))
                v = Vtok[:, t, :].rearrange("p (h v) -> p h v", h=8)
                own(dve.tensor_tensor(v, v, wide(bon[:, t, :], 64), ALU.mult))
                own(dve.tensor_tensor(Obuf[:, t, :], Obuf[:, t, :], Vtok[:, t, :], ALU.add))
                tell(dve.tensor_tensor(Obuf[:, t, :], Obuf[:, t, :], gtok[:, t, :], ALU.mult), "rw")
            dve.wait_ge(sem("d_mb"), 144)
            for t in range(TT):
                s = min(t, 1)
                dve.wait_ge(sem("ysq"), 2 * t + 2)
                tell(dve.tensor_tensor(ssy[:, t:t + 1], ssh[:, 2 * t:2 * t + 1], ssh[:, 2 * t + 1:2 * t + 2],
                                       ALU.add), "yss")
                dve.wait_ge(sem("yrt"), t + 1)
                own(dve.reciprocal(ry[:, t:t + 1], ry[:, t:t + 1]))
                tell(dve.scalar_tensor_tensor(out=h2[:, t, :], in0=ps[:, 2 * t:2 * t + 2, :].rearrange("p a n -> p (a n)"),
                                              scalar=ry[:, t:t + 1], in1=MB[:, 0, s, :], op0=ALU.mult,
                                              op1=ALU.mult), "y_ev")
                tell(dve.tensor_tensor(res[:, t, :], res[:, t, :], h2[:, t, :], ALU.add), "x1")
                dve.wait_ge(sem("xrt"), t + 1)
                own(dve.reciprocal(rx[:, t:t + 1], rx[:, t:t + 1]))
                own(dve.scalar_tensor_tensor(out=h2[:, t, :], in0=res[:, t, :], scalar=rx[:, t:t + 1],
                                             in1=MB[:, 1, s, :], op0=ALU.mult, op1=ALU.mult))
                tell(dve.tensor_tensor(h2[:, t, :], h2[:, t, :], MB[:, 2, s, :], ALU.add), "h2")
            dve.wait_ge(sem("route"), 2)
            dve.wait_ge(sem("d_route"), 64)
            own(dve.tensor_tensor(biased, scores, rep(rbias, TT), ALU.add))
            for t in range(TT):
                for g in range(8):
                    ins = dve.max(m8[:, t, g, :], biased[:, t, 8 * g:8 * g + 8])
            own(ins)
            own(dve.tensor_tensor(grp, m8[:, :, :, 0], m8[:, :, :, 1], ALU.add))
            for t in range(TT):
                own(dve.max(gm[:, t, :], grp[:, t, :]))
                own(dve.max_index(gi[:, t, :], gm[:, t, :], grp[:, t, :]))
            own(dve.tensor_copy(gif, gi))
            for t in range(TT):
                own(dve.tensor_tensor(eq[:, t], wide(iota[:, 0:8], 4), rep(gif[:, t, 0:4], 8), ALU.is_equal))
                own(dve.tensor_reduce(gmask[:, t, :], eq[:, t], AX.X, ALU.add))
            own(dve.tensor_scalar(gneg, gmask, -1.0, 1e30, ALU.add, ALU.mult))
            for t in range(TT):
                b8 = biased[:, t, :].rearrange("p (g e) -> p g e", g=8)
                own(dve.tensor_tensor(b8, b8, wide(gmask[:, t, :], 8), ALU.mult))
                own(dve.tensor_tensor(b8, b8, wide(gneg[:, t, :], 8), ALU.add))
                own(dve.max(em[:, t, :], biased[:, t, :]))
                own(dve.max_index(ei[:, t, :], em[:, t, :], biased[:, t, :]))
            own(dve.tensor_copy(eif, ei))
            for t in range(TT):
                own(dve.tensor_tensor(oh[:, t], rep(iota, TOP_K), wide(eif[:, t, 0:TOP_K], E_N), ALU.is_equal))
                ins = dve.tensor_reduce(emask[:, t, :], oh[:, t].rearrange("p k e -> p e k"), AX.X, ALU.add)
                if t < TT - 1:
                    own(ins)
                else:
                    ins.then_inc(sem("route"), 1)
            for t in range(TT):
                own(dve.tensor_tensor(oht[:, t], oh[:, t], rep(scores[:, t, :], TOP_K), ALU.mult))
                own(dve.tensor_reduce(gk[:, t, :], oht[:, t], AX.X, ALU.add))
            own(dve.tensor_reduce(wsum, gk, AX.X, ALU.add))
            own(dve.reciprocal(wsum, wsum))
            own(dve.tensor_scalar(wsum, wsum, ROUTED_SCALE, None, ALU.mult))
            own(dve.tensor_tensor(rec[:, :, 2].bitcast(F32).rearrange("p (t k) -> p t k", t=TT), gk,
                                  wide(wsum, TOP_K), ALU.mult))
            dve.wait_ge(sem("route"), 4)
            own(dve.scalar_tensor_tensor(out=posx, in0=ps[:, 1, 0:TT * E_N].rearrange("p (t e) -> p t e", t=TT),
                                         scalar=float(E_N), in1=rep(iota, TT), op0=ALU.mult, op1=ALU.add))
            for t in range(TT):
                own(dve.tensor_tensor(oht[:, t], oh[:, t], rep(posx[:, t, :], TOP_K), ALU.mult))
                own(dve.tensor_reduce(dest[:, t, :], oht[:, t], AX.X, ALU.add))
            d2 = dest.rearrange("p t k -> p (t k)")
            dve.tensor_copy(desti, d2).then_inc(sem("route"), 1)
            dve.tensor_reduce(flagc, d2, AX.X, ALU.max).then_inc(sem("route"), 1)
            for t in range(1, TT):
                dve.wait_ge(sem("sh_up"), t + 1)
                dve.wait_ge(sem("sh_at"), t)
                dve.tensor_tensor(hid[0], sgl[0], sgl[1], ALU.mult).then_inc(sem("sh_hid"), 1)
            dve.wait_ge(sem("route"), 7)
            own(dve.tensor_reduce(flagc[0:1, :], ps[0:1, 1, 0:P], AX.X, ALU.max))
            dve.tensor_scalar(flagi, flagc[0:1, :], float(OVER), None, ALU.is_ge).then_inc(sem("route"), 1)

            def hidden(u, e):
                dve.wait_ge(sem("sg"), e + 1)
                if not (isinstance(e, int) and e < 2):
                    dve.wait_ge(sem("at2"), e - 1)
                dve.tensor_tensor(hid[u % 2], sgl[u % 2], ps[:, 2 + u % 2, FF:2 * FF], ALU.mult
                                  ).then_inc(sem("hid"), 1)

            def tokens_t(u, e):
                dve.wait_ge(sem("xt2"), e + 1)
                if not (isinstance(e, int) and e < 2):
                    dve.wait_ge(sem("gu_ps"), e - 1)
                dve.tensor_copy(xgT[u % 2][:, 0:4, :].rearrange("p c t -> p (c t)"), ps[:, 0, :]
                                ).then_inc(sem("xtv"), 1)

            def out_half(u, e, it):
                dve.wait_ge(sem("dn_ps"), e + 1)
                dve.wait_ge(sem("ix"), e * 2 + 4)
                if not (isinstance(e, int) and e < 2):
                    dve.wait_ge(sem(f"d_sc{(u + 2) % 4}"), 16 * (it + (1 if u >= 2 else 0)))
                dve.tensor_scalar(yb[u % 2][:, 0:512], ps[:, 5, :], gate(u), None, ALU.mult).then_inc(sem("yv"), 1)

            def expert(u, e, it, last=False):
                hidden(u, e)
                if not last:
                    tokens_t((u + 1) % 4, e + 1)
                if not (isinstance(e, int) and e == 0):
                    out_half((u + 3) % 4, e - 1, it - (1 if u == 0 else 0))

            dve.wait_ge(sem("sh_y"), TT)
            tokens_t(0, 0)
            for u in range(4):
                expert(u, u, 0)
            with dve.Fori(1, NB - 1) as it:
                for u in range(4):
                    expert(u, it * 4 + u, it)
            for u in range(4):
                expert(u, E_N - 4 + u, NB - 1, last=u == 3)
            out_half(3, E_N - 1, NB - 1)
            dve.wait_ge(sem("route"), 8)
            flag = dve.value_load(flagi[0:1, 0:1], min_val=0, max_val=1)
            with dve.If(flag > 0):
                for b in range(2):
                    with dve.Fori(0, E_N) as e:
                        n = e + b * E_N
                        dve.wait_ge(sem("over"), n * 11 + 5)
                        dve.tensor_tensor(hid[0], sgl[0], ps[:, 2, FF:2 * FF], ALU.mult).then_inc(sem("over"), 1)
            def total(t):
                for k in range(TOP_K):
                    dve.wait_ge(sem(f"d_yk{t}{2 * k // TOP_K}"), 16)
                    ins = dve.tensor_tensor(ysh[:, t, :], ysh[:, t, :], yk[t][:, k * D:(k + 1) * D], ALU.add)
                    own(ins) if k < TOP_K - 1 else tell(ins, "moe")

            def final(t):
                s = min(t, 1)
                dve.wait_ge(sem("xrt"), TT + t + 1)
                own(dve.reciprocal(rx[:, t:t + 1], rx[:, t:t + 1]))
                own(dve.scalar_tensor_tensor(out=ysh[:, t, :], in0=ysh[:, t, :], scalar=rx[:, t:t + 1],
                                             in1=Gf[:, s, :], op0=ALU.mult, op1=ALU.mult))
                tell(dve.tensor_tensor(res[:, t, :], res[:, t, :], ysh[:, t, :], ALU.add), "fin")

            total(0)
            total(1)
            dve.wait_ge(sem("d_gf"), 32)
            final(0)
            total(2)
            final(1)
            final(2)

        @block.tensor
        def _(pe):
            ident = cst("ident")

            def mm(out, lhsT, rhs, start=True, stop=True):
                return pe.matmul(out, lhsT, rhs, start=start, stop=stop, skip_group_check=True)

            def tr(out, in_, n=P):
                return pe.transpose(out, in_, ident[0:n, 0:n])

            def ada(n):
                if n == 0:
                    pe.wait_ge(sem("csil"), 1)
                pe.wait_ge(sem(f"d_ada{n % 3}"), 32 * (n // 3 + 1))
                if n >= 2:
                    pe.wait_ge(sem("mod_ev"), n - 1)
                for c in range(KC):
                    ins = mm(ps[0:2, n % 2, :], csil[:, c, :], ring[n % 3][:, c, :], c == 0, c == KC - 1)
                ins.then_inc(sem("ada_ps"), 1)

            def z(i):
                b = ps[:, 2 + i % 6, :]
                if i >= 6:
                    pe.wait_ge(sem("z_act"), i - 5)
                    if i - 6 < NZ:
                        pe.wait_ge(sem("z_dve"), i - 5)
                if i < I_DI or I_ATT <= i < I_V:
                    if i < I_DI:
                        ch, n = divmod(i, 5)
                        if ch == 0:
                            n = i
                    else:
                        ch, n = 3, i - I_ATT
                    pe.wait_ge(sem(f"d_win{ch}"), 16)
                    for c in range(KC):
                        ins = mm(b[:, 0:T], w_chunk[ch][:, c, n * P:(n + 1) * P], hT[:, c, :], c == 0, c == KC - 1)
                elif i < I_ATT:
                    a, dj = divmod(i - I_DI, 8)
                    d, j = divmod(dj, 4)
                    pe.wait_ge(sem("d_early"), 96)
                    pe.wait_ge(sem("lowr"), 1)
                    r = slice(64 * d, 64 * d + 64)
                    ins = mm(b[:, 0:T], (w2d, w2a)[a][r, j * P:(j + 1) * P], zs[r, 12 + a, :])
                else:
                    for t in range(TT):
                        for c in range(KC):
                            ins = mm(b[:, t * P:(t + 1) * P], hT[:, c, t * P:(t + 1) * P],
                                     w_chunk[3][:, c, 5 * P:6 * P], c == 0, c == KC - 1)
                ins.then_inc(sem("z_ps"), 1)

            for n in range(8):
                ada(n)
            pe.wait_ge(sem("d_const"), 32)
            for t in range(TT):
                pe.wait_ge(sem("xn"), t + 1)
                pe.wait_ge(sem("ss"), 3)
                for hf in range(2):
                    for c in range(4):
                        k = 4 * hf + c
                        ins = tr(ps[:, 2 + 2 * t + hf, c * P:(c + 1) * P], xin[:, t, k:D:KC])
                    ins.then_inc(sem("xt_ps"), 1)
            pe.wait_ge(sem("ht_dve"), 3)
            pe.wait_ge(sem("ht_act"), 3)
            for i in range(I_ATT):
                z(i)
            ada(8)
            ada(9)
            for i in range(I_ATT, I_END):
                z(i)
            ada(10)
            ada(11)
            pe.wait_ge(sem("sq"), 9)
            pe.wait_ge(sem("mod_ev"), 12)
            hsum = erl("hsum").rearrange("p (j m) -> p j m", j=9)
            hbc = erl("hbc").rearrange("p (j m) -> p j m", j=9)
            for j in range(9):
                ins = mm(ps[0:18, 0, 0:T], hsum[:, j, :], sq9[:, j, :], j == 0, j == 8)
            ins.then_inc(sem("nrm"), 1)
            pe.wait_ge(sem("nrm"), 3)
            pe.wait_ge(sem("z_act"), I_END)
            for j in range(9):
                if j >= 6:
                    pe.wait_ge(sem("hb_ev"), j - 5)
                mm(ps[:, 2 + j % 6, 0:T], hbc[0:18, j, :], rs18).then_inc(sem("hb_ps"), 1)
            for j in range(5):
                pe.wait_ge(sem("hb_ev"), j + 1)
                if j >= 2:
                    pe.wait_ge(sem("rp_ev"), j - 1)
                mm(ps[:, j % 2, 0:T], erl("rot"), raw[:, j, :]).then_inc(sem("rp_ps"), 1)
            pe.wait_ge(sem("hb_ev"), 9)
            for t in range(TT):
                for j in range(4):
                    ins = tr(ps[:, 4 + t, j * P:(j + 1) * P], zs[:, 8 + j, t * P:(t + 1) * P])
                ins.then_inc(sem("vt_ps"), 1)
            pe.wait_ge(sem("d_early"), 96)
            tr(ps[:, 7, 0:P], raw[:, 4, 0:P])
            tr(ps[:, 7, P:2 * P], ck).then_inc(sem("ko_ps"), 1)
            pe.wait_ge(sem("rope"), 6)
            pe.wait_ge(sem("kown"), 2)
            for kv in range(2):
                mm(ps[:, 2 + kv, :], erl(f"dup{kv}"), kall).then_inc(sem("dup_ps"), 1)
            for t in range(TT):
                pe.wait_ge(sem("vt_ev"), t + 1)
                mm(ps[:, 4 + t, :], zs[:, 14, t * P:(t + 1) * P], g2).then_inc(sem("vt_ps"), 1)
            pe.wait_ge(sem("dup_ev"), 2)
            pe.wait_ge(sem("rp_ev"), 5)
            pe.wait_ge(sem("rope"), 6)
            n_pt = 0
            for g in range(6):
                qt, kv = divmod(g, 2)
                keys = slice(0, P) if qt == 0 else slice(P, 4 * P)
                nk = 1 if qt == 0 else 3
                for i in range(4):
                    if g:
                        pe.wait_ge(sem("ex"), 4 * (g - 1) + i + 1)
                    h = 4 * kv + i
                    r = slice(64 * (h % 2), 64 * (h % 2) + 64)
                    mm(ps[:, i, 0:nk * P], qr[r, h // 2, qt * P:(qt + 1) * P], kdup[r, kv, keys]
                       ).then_inc(sem("sc_ps"), 1)
                pe.wait_ge(sem("vt_ev"), 2 * TT)
                if n_pt:
                    pe.wait_ge(sem("pt_ev"), n_pt)
                for i in range(4):
                    pe.wait_ge(sem("pn"), 4 * g + i + 1)
                    for kt in range(nk):
                        ins = tr(ps[:, 4 + kt, i * P:(i + 1) * P], Pb[:, i, kt * P:(kt + 1) * P])
                ins.then_inc(sem("pt_ps"), 1)
                n_pt += nk
                pe.wait_ge(sem("pt_ev"), n_pt)
                if g:
                    pe.wait_ge(sem("at_ev"), g)
                for par in range(2):
                    for kt in range(nk):
                        v = vown[:, 0, :] if qt == 0 else (cv if kt == 0 else vown[:, kt, :])
                        pr = PTb[:, kt, :].rearrange("p (a b t) -> p a b t", a=2, b=2)[:, :, par, :]
                        ins = mm(ps[64 * par:64 * par + 64, 7, 0:2 * P], v[:, 64 * kv:64 * kv + 64], pr,
                                 kt == 0, kt == nk - 1)
                ins.then_inc(sem("pv_ps"), 1)
            pe.wait_ge(sem("prep"), 4)
            pe.wait_ge(sem("zero"), 3)
            pe.wait_ge(sem("at_ev"), 6)

            for p in range(3):
                for d in range(2):
                    blk = BLOCKS[d][p]
                    ts = slice(blk * P, (blk + 1) * P)
                    for k, (lh, rh) in enumerate(((bM, aM), (kM, aM), (bM, rM), (kM, rM))):
                        for par in range(2):
                            r = slice(64 * par, 64 * par + 64)
                            if d == 0 and p:
                                if k == 0:
                                    pe.wait_ge(sem("o_ev"), 2 * p)
                                if k == 3:
                                    pe.wait_ge(sem("s_ev"), 2 * p)
                            if d == 1 and k == 0:
                                pe.wait_ge(sem("lt_ev"), 4 * p + par + 1)
                            elif d == 1:
                                pe.wait_ge(sem("m_ev"), 12 * p + 2 * (k - 1) + par + 1)
                            for j in range(4):
                                ins = mm(ps[:, 2 * k + par, j * P:(j + 1) * P], lh[r, 4 * d + j, ts], rh[r, 4 * d + j, ts])
                            ins.then_inc(sem("lt_ps") if k == 0 else sem("m_ps"), 1)
                if p == 1:
                    pe.wait_ge(sem("lt_ev"), 8)
                    for t in range(TT):
                        for j in range(4):
                            ins = mm(ps[:, 0, t * 8 + 2 * j:t * 8 + 2 * j + 2], zs[:, 4 + j, t * P:(t + 1) * P], cst("bones"))
                    ins.then_inc(sem("bon_ps"), 1)
                pe.wait_ge(sem("m_ev"), 12 * p + 12)
                for d in range(2):
                    pe.wait_ge(sem("y2"), 4 * p + 2 * d + 2)
                    for u in range(8):
                        ins = tr(ps[:, 4 * d + 2 + u // 4, (u % 4) * P:(u % 4 + 1) * P], Y[d][:, u, :])
                        if u % 4 == 3:
                            ins.then_inc(sem("t_ps"), 1)
                pe.wait_ge(sem("lt_ev"), 4 * p + 4)
                if p == 1:
                    for d in range(2):
                        for j in range(4):
                            ins = tr(ps[:, 4 * d + 1, j * P:(j + 1) * P], Sp[d][:, j, :])
                        ins.then_inc(sem("so_ps"), 1)
                for l, s in enumerate(LEVELS):
                    if l == 0 and p == 1:
                        pe.wait_ge(sem("bon_ev"), 1)
                    for d in range(2):
                        if l == 0:
                            pe.wait_ge(sem("t_ev"), 28 * p + 2 * d + 2)
                        for u in range(8):
                            xs = X[d][:, u, :].rearrange("p (n a s) -> p n a s", a=2, s=s)[:, :, d, :]
                            ins = mm(ps[:, 4 * d, u * 64:(u + 1) * 64], LT[d][:, u, :], xs)
                        ins.then_inc(sem("h_ps"), 1)
                    for d in range(2):
                        pe.wait_ge(sem("h_ev"), 12 * p + 2 * l + d + 1)
                        if l:
                            pe.wait_ge(sem("t_ev"), 28 * p + 4 * l + 2 * d + 2)
                        elif p == 1:
                            pe.wait_ge(sem("st_out"), d + 1)
                        for u in range(8):
                            ins = mm(ps[:, 4 * d + 1, u * 64:(u + 1) * 64], Y[d][:, u, :], Hs[d][:, u, :])
                        ins.then_inc(sem("zz_ps"), 1)
                    for d in range(2):
                        pe.wait_ge(sem("x_ev"), 12 * p + 2 * l + d + 1)
                        for u in range(8):
                            ins = tr(ps[:, 4 * d + 2 + u // 4, (u % 4) * P:(u % 4 + 1) * P], X[d][:, u, :])
                            if u % 4 == 3:
                                ins.then_inc(sem("t_ps"), 1)
                pe.wait_ge(sem("t_ev"), 28 * p + 28)
                if p == 1:
                    pe.wait_ge(sem("d_state"), 64)
                    for d in range(2):
                        for j in range(4):
                            ins = tr(ps[:, 6 + d, j * P:(j + 1) * P], SD[d][:, j, :])
                        ins.then_inc(sem("sd_ps"), 1)
                    pe.wait_ge(sem("sp"), 2)
                if p == 2:
                    pe.wait_ge(sem("s_ev"), 4)
                tss = [slice(BLOCKS[d][p] * P, (BLOCKS[d][p] + 1) * P) for d in range(2)]
                for d in range(2):
                    blk, ts = BLOCKS[d][p], tss[d]
                    for j in range(4):
                        if p:
                            mm(ps[:, d, j * P:(j + 1) * P], aM[:, 4 * d + j, ts], Sp[d][:, j, :], True, False)
                        for par in range(2):
                            hv = slice((2 * j + par) * 64, (2 * j + par + 1) * 64)
                            ins = mm(ps[:, d, hv], MT[d][:, 4 * par + j, :], Vtok[:, blk, hv], not p, True)
                    ins.then_inc(sem("w_ps"), 1)
                if p < 2:
                    for d in range(2):
                        for h, m in enumerate((bM, kM)):
                            for j in range(4):
                                ins = tr(ps[:, 6 - 2 * d + h, j * P:(j + 1) * P], m[:, 4 * d + j, tss[d]])
                            ins.then_inc(sem("bk_ps"), 1)
                for d in range(2):
                    pe.wait_ge(sem("w_ev"), 2 * p + d + 1)
                    for j in range(4):
                        for par in range(2):
                            hv = slice((2 * j + par) * 64, (2 * j + par + 1) * 64)
                            ins = mm(ps[:, 2 + d, hv], Y[d][:, 4 * par + j, :], Ws[d][:, hv])
                    ins.then_inc(sem("u_ps"), 1)
                for d in range(2):
                    blk, ts = BLOCKS[d][p], tss[d]
                    pe.wait_ge(sem("u_ev"), 2 * p + d + 1)
                    for j in range(4):
                        if p:
                            mm(ps[:, d, j * P:(j + 1) * P], rM[:, 4 * d + j, ts], Sp[d][:, j, :], True, False)
                        for par in range(2):
                            hv = slice((2 * j + par) * 64, (2 * j + par + 1) * 64)
                            mm(ps[:, d, hv], RB[d][:, 4 * par + j, :], Us[d][:, hv], not p, False)
                            ins = mm(ps[:, d, hv], RK[d][:, 4 * par + j, :], Vtok[:, blk, hv], False, True)
                    ins.then_inc(sem("o_ps"), 1)
                if p < 2:
                    for d in range(2):
                        blk = BLOCKS[d][p]
                        pe.wait_ge(sem("bk_ev"), 4 * p + 2 * d + 2)
                        for j in range(4):
                            js = slice(j * P, (j + 1) * P)
                            mm(ps[:, 6 + d, js], bktok[d][:, j, :], Us[d][:, js], True, False)
                            ins = mm(ps[:, 6 + d, js], bktok[d][:, 4 + j, :], Vtok[:, blk, js], False, True)
                        ins.then_inc(sem("s_ps"), 1)
            pe.wait_ge(sem("o_ev"), 6)
            def project(t, half):
                src, w = ((attnT, woA), (rwT, woR))[half]
                for hf in range(2):
                    for c in range(4):
                        ins = mm(ps[:, 2 * t + hf, :], src[:, c, t * P:(t + 1) * P],
                                 w[:, c, hf * 512:(hf + 1) * 512], half == 0 and c == 0, half == 1 and c == 3)
                return ins

            pe.wait_ge(sem("d_wo"), 32)
            for t in range(TT):
                project(t, 0)
                pe.wait_ge(sem("rw"), t + 1)
                if t == 2:
                    pe.wait_ge(sem("rw_ev"), 1)
                for j in range(4):
                    ins = tr(ps[:, 6 + t % 2, j * P:(j + 1) * P], Obuf[:, t, j * P:(j + 1) * P])
                ins.then_inc(sem("rw_ps"), 1)
            rwv = rw_sb.rearrange("p (c e) -> p c e", c=KC)

            def logits(t):
                pe.wait_ge(sem("ht2_ev"), 2 * t + 2)
                for c in range(KC):
                    ins = mm(ps[:, 0, t * E_N:(t + 1) * E_N], h2T[:, c, t * P:(t + 1) * P], rwv[:, c, :],
                             c == 0, c == KC - 1)
                return ins

            def transposed(t):
                pe.wait_ge(sem("h2"), t + 1)
                for hf in range(2):
                    if t:
                        pe.wait_ge(sem("ht2_ev"), 2 * (t - 1) + hf + 1)
                    for c in range(4):
                        ins = tr(ps[:, 6 + hf, c * P:(c + 1) * P], h2[:, t, 4 * hf + c:D:KC])
                    ins.then_inc(sem("ht2_ps"), 1)

            def up(bank, xT, w, name):
                for c in range(KC):
                    ins = mm(ps[:, bank, :], xT[:, c, :], w[:, c, :], c == 0, c == KC - 1)
                ins.then_inc(sem(name), 1)

            def hid_t(bank, h, name):
                for c in range(2):
                    ins = tr(ps[:, bank, c * P:(c + 1) * P], h[:, c:FF:2])
                ins.then_inc(sem(name), 1)

            def down(bank, hT_, w, name):
                for hf in range(2):
                    for c in range(2):
                        ins = mm(ps[:, bank + hf, :], hT_[:, c, :], w[:, c, hf * 512:(hf + 1) * 512], c == 0, c == 1)
                ins.then_inc(sem(name), 1)

            def positions():
                pe.wait_ge(sem("route"), 3)
                for t in range(TT):
                    b = ps[:, 1, t * E_N:(t + 1) * E_N]
                    ins = mm(b, cst("st0"), emask[:, t, :], True, t == 0)
                    for s in range(t):
                        ins = mm(b, cst("ones"), emask[:, s, :], False, s == t - 1)
                ins.then_inc(sem("route"), 1)

            for t in range(TT):
                pe.wait_ge(sem("rw_ev"), t + 1)
                project(t, 1).then_inc(sem("y_ps"), 1)
                if t:
                    pe.wait_ge(sem("rw_ev"), TT)
                    transposed(t - 1)
            pe.wait_ge(sem("d_route"), 64)
            pe.wait_ge(sem("y_ev"), 2)
            logits(0)
            logits(1)
            pe.wait_ge(sem("d_shared"), 32)
            up(2, h2T[:, :, 0:P], s13(3), "sh_gu")
            transposed(2)
            logits(2).then_inc(sem("route"), 1)
            pe.wait_ge(sem("y_ev"), TT)
            for t in range(TT):
                pe.wait_ge(sem("sh_hid"), t + 1)
                hid_t(3, hid[0], "sh_at")
                if t == 0:
                    positions()
                if t < TT - 1:
                    up(2, h2T[:, :, (t + 1) * P:(t + 2) * P], s13(3), "sh_gu")
                pe.wait_ge(sem("sh_att"), t + 1)
                if t:
                    pe.wait_ge(sem("sh_y"), t)
                down(4, hidT[0], sd(3), "shared_ps")
            pe.wait_ge(sem("route"), 6)
            tr(ps[0:1, 1, 0:P], flagc).then_inc(sem("route"), 1)
            pe.wait_ge(sem("route"), 8)
            pe.wait_ge(sem("sh_y"), TT)

            def tokens_t(u, e, it):
                pe.wait_ge(sem(f"d_xg{u}"), 16 * (it + 1))
                if not (isinstance(e, int) and e == 0):
                    pe.wait_ge(sem("xtv"), e)
                    pe.wait_ge(sem("xta"), e)
                for c in range(KC):
                    ins = tr(ps[:, c // 4, (c % 4) * P:(c % 4 + 1) * P], xg[u][:, c:D:KC])
                ins.then_inc(sem("xt2"), 1)

            def expert(u, e, it, last=False):
                pe.wait_ge(sem("xtv"), e + 1)
                pe.wait_ge(sem("xta"), e + 1)
                pe.wait_ge(sem(f"d_we{u}"), 32 * (it + 1))
                if not (isinstance(e, int) and e < 2):
                    pe.wait_ge(sem("hid"), e - 1)
                up(2 + u % 2, xgT[u % 2], s13(u), "gu_ps")
                if not last:
                    tokens_t((u + 1) % 4, e + 1, it + (1 if u == 3 else 0))
                if not (isinstance(e, int) and e == 0):
                    finish((u + 3) % 4, e - 1, it - (1 if u == 0 else 0))
                pe.wait_ge(sem("hid"), e + 1)
                hid_t(4, hid[u % 2], "at2")

            def finish(u, e, it):
                pe.wait_ge(sem("hta"), e + 1)
                if not (isinstance(e, int) and e == 0):
                    pe.wait_ge(sem("yv"), e)
                    pe.wait_ge(sem("ya"), e)
                down(5, hidT[u % 2], sd(u), "dn_ps")

            tokens_t(0, 0, 0)
            for u in range(4):
                expert(u, u, 0)
            with pe.Fori(1, NB - 1) as it:
                for u in range(4):
                    expert(u, it * 4 + u, it)
            for u in range(4):
                expert(u, E_N - 4 + u, NB - 1, last=u == 3)
            finish(3, E_N - 1, NB - 1)
            pe.wait_ge(sem("route"), 8)
            flag = pe.value_load(flagi[0:1, 0:1], min_val=0, max_val=1)
            with pe.If(flag > 0):
                pe.wait_ge(sem("yv"), E_N)
                pe.wait_ge(sem("ya"), E_N)
                for b in range(2):
                    with pe.Fori(0, E_N) as e:
                        n = e + b * E_N
                        pe.wait_ge(sem("d_ovx"), n * 32 + 16)
                        for c in range(KC):
                            ins = tr(ps[:, c // 4, (c % 4) * P:(c % 4 + 1) * P], xg[0][:, c:D:KC])
                        ins.then_inc(sem("over"), 1)
                        pe.wait_ge(sem("over"), n * 11 + 3)
                        pe.wait_ge(sem("d_ov"), (n + 1) * 32)
                        up(2, xgT[0], s13(0), "over")
                        pe.wait_ge(sem("over"), n * 11 + 6)
                        hid_t(4, hid[0], "over")
                        pe.wait_ge(sem("over"), n * 11 + 8)
                        down(5, hidT[0], sd(0), "over")


def host_layout(inputs):
    f = {k: np.ascontiguousarray(np.asarray(v)) for k, v in inputs.items()}
    main, early = constant_arrays()

    def tiles(v, n):
        return v.reshape(n, P).T

    a = {"c_main": main, "c_early": early}
    a["x"] = np.concatenate([f["x_prompt"][0], f["x_sample"][0]], 0)
    a["cvec"] = np.stack([f["c_ctx"], f["c"][0]], 0).reshape(2, P, KC).transpose(1, 2, 0).reshape(P, 2 * KC)
    a["cols"] = np.concatenate([
        f["g_pre_mix"][0].reshape(P, KC),
        np.concatenate([f["q_gain"][0]] * 2)[:, None], np.concatenate([f["k_gain"][0]] * 2)[:, None],
        tiles(f["mu_prev"][0], NZ), tiles(f["mu_next"][0], NZ),
        tiles(f["decay_w0"][0], 8), tiles(f["iclr_a0"][0], 8),
        tiles(f["k_k"][0], 4), tiles(f["k_a"][0], 4), tiles(f["r_k"][0], 4)], 1)
    zero = np.zeros(D, np.float32)
    gains = np.stack([zero, zero, f["g_post_mix"][0], zero, f["g_pre_ffn"][0], f["g_post_ffn"][0]])
    a["adarows"] = np.stack([f["b_ada"][0].reshape(12, 512), gains.reshape(12, 512)], 1).reshape(12, 1024)
    a["w_ada"], a["w_in"], a["w_out"] = f["w_ada"][0], f["w_in"][0], f["w_out"][0]
    a["decay_w2"] = f["decay_w2"][0].reshape(P, 512)
    a["iclr_a2"] = f["iclr_a2"][0].reshape(P, 512)
    a["gate_g2"] = f["gate_g2"][0]
    a["cache_k"] = f["cache_k"][0, 0].reshape(P, P)
    a["cache_v"] = f["cache_v"][0, 0].reshape(P, P)
    a["state"] = f["state_rwkv"][0, 0].reshape(2, 4, 2, 64, 64).transpose(0, 2, 3, 1, 4)
    a["lnx_g"], a["lnx_b"] = f["lnx_g"][0], f["lnx_b"][0]
    a["router_w"] = f["router_w"][0].reshape(P, KC * E_N)
    a["router_b"] = f["router_b"][0]
    a["w13"] = np.concatenate([f["expert_wg"][0], f["expert_wu"][0]], -1).reshape(E_N, P, KC * 2 * FF)
    a["wd"] = f["expert_wd"][0].reshape(E_N, P, 2 * D)
    a["shared13"] = np.concatenate([f["shared_wg"][0], f["shared_wu"][0]], -1).reshape(P, KC * 2 * FF)
    a["shared_wd"] = f["shared_wd"][0].reshape(P, 2 * D)
    a["c_iota"] = np.tile(np.arange(E_N, dtype=np.float32), (P, 1))
    rec = np.zeros((P, TT, TOP_K, 4), np.int32)
    token = np.arange(T, dtype=np.int32).reshape(TT, P).T
    rec[..., 0] = token[:, :, None] * TOP_K + np.arange(TOP_K, dtype=np.int32)
    rec[..., 1] = token[:, :, None]
    a["c_rec"] = rec.reshape(P, -1)
    a["c_list"] = np.tile(np.array([BIG, BIG, 0, 0], np.int32), (T * E_N, 1))
    return {k: np.ascontiguousarray(v) for k, v in a.items()}


OUTS = [("y", (T, D)), ("cache_k", (P, P)), ("cache_v", (P, P)), ("state", (2, 2, 64, 4, 64))]


def kernel(**inputs):
    import concourse.bacc as _bacc
    from concourse.bass_utils import run_bass_kernel_spmd as _run

    nc = _bacc.Bacc("TRN2", target_bir_lowering=False, num_devices=1)
    arrays, ins, outs = {}, {}, {}
    for name, a in host_layout(inputs).items():
        arrays[f"in_{name}"] = a
        ins[name] = nc.dram_tensor(f"in_{name}", a.shape, mybir.dt.from_np(a.dtype), kind="ExternalInput").ap()
    for name, shape in OUTS:
        outs[name] = nc.dram_tensor(f"out_{name}", shape, F32, kind="ExternalOutput").ap()
    program(nc, ins, outs)
    r = _run(nc, [arrays], core_ids=[0]).results[0]
    y = r["out_y"]
    st = r["out_state"].transpose(0, 3, 1, 2, 4).reshape(1, 1, 2, 8, 64, 64)
    return (y[None, :P], y[None, P:], r["out_cache_k"].reshape(1, 1, P, 2, 64),
            r["out_cache_v"].reshape(1, 1, P, 2, 64), st)
```
